# Optimizing a Trainium2 kernel written in Bass

```python
import math
import jax, jax.numpy as jnp
from jax import lax
import numpy as np

D_MODEL = 1024
BATCH = 1
SEQ = 256
DEPTH = 1

ATTN_HEADS = 8
ATTN_KV_GROUPS = 2
HEAD_DIM = 64
IDX_HEADS = 4
IDX_DIM = 64
TOPK_MAX = 256
Q_BLOCK = 128
NUM_BUCKETS = 32
MAX_DISTANCE = 128
HGRN_HEADS = 4
HGRN_DIM = 128
HGRN_CHUNK = 64
CONV_W = 512
CONV_K = 3
D_FF = 4 * D_MODEL

ATTN_W = ATTN_HEADS * HEAD_DIM
KV_W = ATTN_KV_GROUPS * HEAD_DIM
HGRN_W = HGRN_HEADS * HGRN_DIM
N_BRANCH = 3
EPS = 1e-6
SPLITS = (ATTN_W, KV_W, KV_W,
          IDX_HEADS * IDX_DIM, IDX_DIM, IDX_HEADS,
          HGRN_W, HGRN_W, HGRN_W, HGRN_W,
          CONV_W, CONV_W, CONV_W,
          N_BRANCH * D_MODEL)
D_IN_PROJ = sum(SPLITS)


def _rmsnorm(x, g):
    xf = x.astype(jnp.float32)
    y = xf * lax.rsqrt(jnp.mean(xf * xf, axis=-1, keepdims=True) + EPS)
    return (y * g.astype(jnp.float32)).astype(x.dtype)

def _split_cols(p):
    offs, acc = [], 0
    for w in SPLITS[:-1]:
        acc += w
        offs.append(acc)
    return jnp.split(p, offs, axis=-1)

def _t5_bucket(dist):
    max_exact = NUM_BUCKETS // 2
    d = jnp.maximum(dist, 0)
    df = jnp.maximum(d, 1).astype(jnp.float32)
    large = max_exact + (jnp.log(df / max_exact) / math.log(MAX_DISTANCE / max_exact)
                         * (NUM_BUCKETS - max_exact)).astype(jnp.int32)
    large = jnp.minimum(large, NUM_BUCKETS - 1)
    return jnp.where(d < max_exact, d, large)

def _dsa_attention(q, k, v, qi, ki, wi, rel_bias):
    b, s = q.shape[0], q.shape[1]
    n_sel = min(TOPK_MAX, s // 4)
    nb = s // Q_BLOCK
    npg = ATTN_HEADS // ATTN_KV_GROUPS
    scale = HEAD_DIM ** -0.5
    wi = wi * (IDX_HEADS ** -0.5 * IDX_DIM ** -0.5)
    key_pos = jnp.arange(s)
    bidx = jnp.arange(b)[:, None, None]

    def blocks(a):
        return jnp.moveaxis(a.reshape((b, nb, Q_BLOCK) + a.shape[2:]), 1, 0)

    def one_block(args):
        blk, q_b, qi_b, wi_b = args
        t = blk * Q_BLOCK + jnp.arange(Q_BLOCK)
        sc = jax.nn.relu(jnp.einsum('bqhd,bsd->bqhs', qi_b, ki))
        sc = jnp.einsum('bqhs,bqh->bqs', sc, wi_b).astype(jnp.float32)
        causal = key_pos[None, :] <= t[:, None]
        sc = jnp.where(causal[None], sc, -jnp.inf)
        _, idx = lax.top_k(sc, n_sel)
        valid = idx <= t[None, :, None]
        k_sel = k[bidx, idx]
        v_sel = v[bidx, idx]
        qg = q_b.reshape(b, Q_BLOCK, ATTN_KV_GROUPS, npg, HEAD_DIM)
        logits = jnp.einsum('bqgnd,bqkgd->bqgnk', qg, k_sel).astype(jnp.float32) * scale
        bias = rel_bias[_t5_bucket(t[None, :, None] - idx)]
        bias = jnp.moveaxis(bias, -1, 2).reshape(b, Q_BLOCK, ATTN_KV_GROUPS, npg, n_sel)
        logits = jnp.where(valid[:, :, None, None, :], logits + bias.astype(jnp.float32), -jnp.inf)
        p = jax.nn.softmax(logits, axis=-1).astype(v.dtype)
        o = jnp.einsum('bqgnk,bqkgd->bqgnd', p, v_sel)
        return o.reshape(b, Q_BLOCK, ATTN_W)

    out = lax.map(one_block, (jnp.arange(nb), blocks(q), blocks(qi), blocks(wi)))
    return jnp.moveaxis(out, 0, 1).reshape(b, s, ATTN_W)

def _hgrn2(q, f_logit, i, lb):
    b, s = q.shape[0], q.shape[1]
    nc = s // HGRN_CHUNK
    f32 = jnp.float32
    z = f_logit.astype(f32)
    lb = lb.astype(f32).reshape(HGRN_HEADS, HGRN_DIM)
    log_f = jnp.logaddexp(jnp.log(lb), jnp.log1p(-lb) + jax.nn.log_sigmoid(z))
    kk = (1.0 - lb) * jax.nn.sigmoid(-z)

    def chunks(a):
        return a.reshape(b, nc, HGRN_CHUNK, HGRN_HEADS, HGRN_DIM).transpose(1, 0, 3, 2, 4)

    tri = jnp.tril(jnp.ones((HGRN_CHUNK, HGRN_CHUNK), dtype=bool))

    def step(state, inp):
        qc, kc, ic, gc = inp
        G = jnp.cumsum(gc, axis=2)
        diff = G[:, :, :, None, :] - G[:, :, None, :, :]
        decay = jnp.exp(jnp.where(tri[:, :, None], diff, -jnp.inf))
        attn = jnp.einsum('bhtd,bhsd,bhtsd->bhts', qc, kc, decay)
        o = attn @ ic + jnp.einsum('bhtd,bhdv->bhtv', qc * jnp.exp(G), state)
        g_last = G[:, :, -1:, :]
        state = (jnp.exp(g_last[:, :, 0, :, None]) * state
                 + jnp.einsum('bhsd,bhsv->bhdv', kc * jnp.exp(g_last - G), ic))
        return state, o

    s0 = jnp.zeros((b, HGRN_HEADS, HGRN_DIM, HGRN_DIM), f32)
    _, o = lax.scan(step, s0, (chunks(q.astype(f32)), chunks(kk), chunks(i.astype(f32)), chunks(log_f)))
    return o.transpose(1, 0, 3, 2, 4).reshape(b, s, HGRN_HEADS, HGRN_DIM)

def _short_conv(u, w):
    kern = w[:, None, :].astype(u.dtype)
    return lax.conv_general_dilated(u, kern, (1,), [(CONV_K - 1, 0)],
                                    dimension_numbers=('NWC', 'WIO', 'NWC'),
                                    feature_group_count=u.shape[-1])

def first_inputs(seed: int = 0) -> dict:
    key = jax.random.key(seed)
    ks = jax.random.split(key, 16)
    f32 = jnp.float32

    def nrm(k, shape, scale):
        return jax.random.normal(k, shape, f32) * scale

    def gain(k, shape):
        return 1.0 + 0.02 * jax.random.normal(k, shape, f32)

    return {
        'x': nrm(ks[0], (BATCH, SEQ, D_MODEL), 1.0),
        'rel_bias': nrm(ks[1], (NUM_BUCKETS, ATTN_HEADS), 0.5),
        'hgrn_lb': nrm(ks[2], (DEPTH, HGRN_W), 1.0),
        'ln_mix_g': gain(ks[3], (DEPTH, D_MODEL)),
        'w_in': nrm(ks[4], (DEPTH, D_MODEL, D_IN_PROJ), D_MODEL ** -0.5),
        'q_norm_g': gain(ks[5], (DEPTH, HEAD_DIM)),
        'k_norm_g': gain(ks[6], (DEPTH, HEAD_DIM)),
        'hgrn_norm_g': gain(ks[7], (DEPTH, HGRN_DIM)),
        'conv_w': nrm(ks[8], (DEPTH, CONV_K, CONV_W), CONV_K ** -0.5),
        'w_up_attn': nrm(ks[9], (DEPTH, ATTN_W, D_MODEL), ATTN_W ** -0.5),
        'w_up_hgrn': nrm(ks[10], (DEPTH, HGRN_W, D_MODEL), HGRN_W ** -0.5),
        'w_up_conv': nrm(ks[11], (DEPTH, CONV_W, D_MODEL), CONV_W ** -0.5),
        'w_out': nrm(ks[12], (DEPTH, D_MODEL, D_MODEL), D_MODEL ** -0.5),
        'ln_mlp_g': gain(ks[13], (DEPTH, D_MODEL)),
        'w_mlp_up': nrm(ks[14], (DEPTH, D_MODEL, D_FF), D_MODEL ** -0.5),
        'w_mlp_down': nrm(ks[15], (DEPTH, D_FF, D_MODEL), D_FF ** -0.5),
    }

def first_block(x, rel_bias, hgrn_lb, ln_mix_g, w_in, q_norm_g, k_norm_g, hgrn_norm_g,
              conv_w, w_up_attn, w_up_hgrn, w_up_conv, w_out, ln_mlp_g, w_mlp_up, w_mlp_down):
    b, s, _ = x.shape
    lb_all = jnp.cumsum(jax.nn.softmax(hgrn_lb.astype(jnp.float32), axis=0), axis=0)
    lb_all = lb_all - lb_all[0]
    for l in range(DEPTH):
        h = _rmsnorm(x, ln_mix_g[l])
        proj = h @ w_in[l]
        (aq, ak, av, iq, ik, iw, hq, hf, hi, hg, cb, cc, ch, gates) = _split_cols(proj)
        q = _rmsnorm(aq.reshape(b, s, ATTN_HEADS, HEAD_DIM), q_norm_g[l])
        k = _rmsnorm(ak.reshape(b, s, ATTN_KV_GROUPS, HEAD_DIM), k_norm_g[l])
        v = av.reshape(b, s, ATTN_KV_GROUPS, HEAD_DIM)
        y_attn = _dsa_attention(q, k, v, iq.reshape(b, s, IDX_HEADS, IDX_DIM), ik, iw, rel_bias)
        o = _hgrn2(hq.reshape(b, s, HGRN_HEADS, HGRN_DIM), hf.reshape(b, s, HGRN_HEADS, HGRN_DIM),
                   hi.reshape(b, s, HGRN_HEADS, HGRN_DIM), lb_all[l])
        y_hgrn = (_rmsnorm(o, hgrn_norm_g[l]).astype(x.dtype)
                  * jax.nn.silu(hg.reshape(b, s, HGRN_HEADS, HGRN_DIM))).reshape(b, s, HGRN_W)
        y_conv = cb * _short_conv(cc * ch, conv_w[l])
        g = jax.nn.sigmoid(gates.reshape(b, s, N_BRANCH, D_MODEL))
        mixed = (g[:, :, 0] * (y_attn @ w_up_attn[l])
                 + g[:, :, 1] * (y_hgrn @ w_up_hgrn[l])
                 + g[:, :, 2] * (y_conv @ w_up_conv[l]))
        x = x + mixed @ w_out[l]
        h = _rmsnorm(x, ln_mlp_g[l])
        x = x + jnp.square(jax.nn.relu(h @ w_mlp_up[l])) @ w_mlp_down[l]
    return x


DEPTH_2 = 2

CHUNK = 64
QBLOCK = 128
H_FOX = 8
H_CHK = 8
N_LEFT_CHUNKS = 8
BAND = (N_LEFT_CHUNKS + 1) * CHUNK
REL_CLIP = 256
N_REL = CHUNK - 1 + REL_CLIP + 1
FORGET_BIAS = 3.0
H_SB = 8
H_MLA = 8
Q_LORA = 384
KV_LORA = 256
NOPE_DIM = 64
ROPE_DIM = 32
V_DIM = 64
ROPE_THETA = 10000.0
D_FF_2 = 4 * D_MODEL
N_EVEN = (DEPTH_2 + 1) // 2
N_ODD = DEPTH_2 // 2

W_FOX = H_FOX * HEAD_DIM
W_CHK = H_CHK * HEAD_DIM
W_SB = H_SB * HEAD_DIM
W_MLA = H_MLA * V_DIM
SPLIT_AB = [W_FOX, W_FOX, W_FOX, H_FOX, W_CHK, W_CHK, W_CHK]
SPLIT_CD = [W_SB, W_SB, W_SB, Q_LORA, KV_LORA, ROPE_DIM]
IN_AB = sum(SPLIT_AB)
IN_CD = sum(SPLIT_CD)
MIX_AB = W_FOX + W_CHK
MIX_CD = W_SB + W_MLA


def _split(h, sizes):
    return jnp.split(h, np.cumsum(sizes)[:-1].tolist(), axis=-1)

def rmsnorm(x, g):
    xf = x.astype(jnp.float32)
    y = xf * lax.rsqrt(jnp.mean(xf * xf, axis=-1, keepdims=True) + EPS)
    return (y * g.astype(jnp.float32)).astype(x.dtype)

def rope(x, positions):
    half = ROPE_DIM // 2
    inv_freq = ROPE_THETA ** (-jnp.arange(half, dtype=jnp.float32) / half)
    ang = positions.astype(jnp.float32)[..., None] * inv_freq
    cos = jnp.cos(ang)[:, :, None, :]
    sin = jnp.sin(ang)[:, :, None, :]
    x1 = x[..., :half].astype(jnp.float32)
    x2 = x[..., half:].astype(jnp.float32)
    out = jnp.concatenate([x1 * cos - x2 * sin, x2 * cos + x1 * sin], axis=-1)
    return out.astype(x.dtype)

def _sweep_query_blocks(block_fn, seq):
    out = lax.map(block_fn, jnp.arange(seq // QBLOCK))
    nb, b, qb, h, dv = out.shape
    return jnp.moveaxis(out, 0, 1).reshape(b, nb * qb, h, dv)

def fox_attention(q, k, v, log_f):
    seq = q.shape[1]
    scale = HEAD_DIM ** -0.5
    cum = jnp.transpose(jnp.cumsum(log_f, axis=1), (0, 2, 1))
    k_pos = jnp.arange(seq)

    def block(i):
        start = i * QBLOCK
        qb = lax.dynamic_slice_in_dim(q, start, QBLOCK, axis=1)
        cq = lax.dynamic_slice_in_dim(cum, start, QBLOCK, axis=2)
        q_pos = start + jnp.arange(QBLOCK)
        s = jnp.einsum('bqhd,bkhd->bhqk', qb, k).astype(jnp.float32) * scale
        s = s + cq[..., :, None] - cum[..., None, :]
        mask = k_pos[None, :] <= q_pos[:, None]
        p = jax.nn.softmax(jnp.where(mask, s, -jnp.inf), axis=-1)
        return jnp.einsum('bhqk,bkhd->bqhd', p.astype(v.dtype), v)

    return _sweep_query_blocks(block, seq)

def chunked_relpos_attention(q, k, v, rel_bias):
    b, seq, h, d = q.shape
    nc = seq // CHUNK
    left = N_LEFT_CHUNKS * CHUNK
    scale = HEAD_DIM ** -0.5

    def band(t):
        tp = jnp.pad(t, ((0, 0), (left, 0), (0, 0), (0, 0)))
        tp = tp.reshape(b, nc + N_LEFT_CHUNKS, CHUNK, h, d)
        return jnp.concatenate([tp[:, i:i + nc] for i in range(N_LEFT_CHUNKS + 1)], axis=2)

    kb, vb = band(k), band(v)
    qc = q.reshape(b, nc, CHUNK, h, d)
    rel = np.arange(CHUNK)[:, None] + left - np.arange(BAND)[None, :]
    rel_idx = np.clip(rel, -(CHUNK - 1), REL_CLIP) + (CHUNK - 1)
    bias = rel_bias[:, rel_idx].astype(jnp.float32)
    s = jnp.einsum('bcqhd,bckhd->bhcqk', qc, kb).astype(jnp.float32) * scale
    s = s + bias[None, :, None]
    key_abs = jnp.arange(nc)[:, None] * CHUNK - left + jnp.arange(BAND)[None, :]
    valid = (key_abs >= 0)[None, None, :, None, :]
    p = jax.nn.softmax(jnp.where(valid, s, -jnp.inf), axis=-1)
    out = jnp.einsum('bhcqk,bckhd->bcqhd', p.astype(v.dtype), vb)
    return out.reshape(b, seq, h, d)

def stick_breaking_attention(q, k, v):
    seq = q.shape[1]
    scale = HEAD_DIM ** -0.5
    k_pos = jnp.arange(seq)

    def block(i):
        start = i * QBLOCK
        qb = lax.dynamic_slice_in_dim(q, start, QBLOCK, axis=1)
        q_pos = start + jnp.arange(QBLOCK)
        z = jnp.einsum('bqhd,bkhd->bhqk', qb, k).astype(jnp.float32) * scale
        mask = k_pos[None, :] < q_pos[:, None]
        log_beta = jax.nn.log_sigmoid(z)
        log_keep = jnp.where(mask, jax.nn.log_sigmoid(-z), 0.0)
        suffix = lax.cumsum(log_keep, axis=3, reverse=True) - log_keep
        a = jnp.where(mask, jnp.exp(log_beta + suffix), 0.0)
        return jnp.einsum('bhqk,bkhd->bqhd', a.astype(v.dtype), v)

    return _sweep_query_blocks(block, seq)

def mla_attention(q_nope, q_rope, k_nope, k_rope, v):
    seq = q_nope.shape[1]
    scale = (NOPE_DIM + ROPE_DIM) ** -0.5
    k_chunk = jnp.arange(seq) // CHUNK

    def block(i):
        start = i * QBLOCK
        qn = lax.dynamic_slice_in_dim(q_nope, start, QBLOCK, axis=1)
        qr = lax.dynamic_slice_in_dim(q_rope, start, QBLOCK, axis=1)
        q_chunk = (start + jnp.arange(QBLOCK)) // CHUNK
        s = (jnp.einsum('bqhd,bkhd->bhqk', qn, k_nope)
             + jnp.einsum('bqhr,bkr->bhqk', qr, k_rope)).astype(jnp.float32) * scale
        mask = k_chunk[None, :] <= q_chunk[:, None]
        p = jax.nn.softmax(jnp.where(mask, s, -jnp.inf), axis=-1)
        return jnp.einsum('bhqk,bkhd->bqhd', p.astype(v.dtype), v)

    return _sweep_query_blocks(block, seq)

def even_mixer(h, w_in, b_forget, rel_bias, w_out):
    b, s, _ = h.shape
    qa, ka, va, fa, qb, kb, vb = _split(h @ w_in, SPLIT_AB)
    heads = lambda t, n: t.reshape(b, s, n, HEAD_DIM)
    log_f = jax.nn.log_sigmoid((fa + b_forget).astype(jnp.float32))
    o_a = fox_attention(heads(qa, H_FOX), heads(ka, H_FOX), heads(va, H_FOX), log_f)
    o_b = chunked_relpos_attention(heads(qb, H_CHK), heads(kb, H_CHK), heads(vb, H_CHK), rel_bias)
    o = jnp.concatenate([o_a.reshape(b, s, W_FOX), o_b.reshape(b, s, W_CHK)], axis=-1)
    return o @ w_out

def odd_mixer(h, positions, w_in, q_norm, kv_norm, w_uq, w_ukv, w_out):
    b, s, _ = h.shape
    qc, kc, vc, c_q, c_kv, k_r = _split(h @ w_in, SPLIT_CD)
    heads = lambda t, n, d: t.reshape(b, s, n, d)
    o_c = stick_breaking_attention(heads(qc, H_SB, HEAD_DIM), heads(kc, H_SB, HEAD_DIM), heads(vc, H_SB, HEAD_DIM))
    q_full = heads(rmsnorm(c_q, q_norm) @ w_uq, H_MLA, NOPE_DIM + ROPE_DIM)
    q_nope, q_rope = q_full[..., :NOPE_DIM], rope(q_full[..., NOPE_DIM:], positions)
    kv_full = heads(rmsnorm(c_kv, kv_norm) @ w_ukv, H_MLA, NOPE_DIM + V_DIM)
    k_nope, v_d = kv_full[..., :NOPE_DIM], kv_full[..., NOPE_DIM:]
    k_rope = rope(k_r[:, :, None, :], positions)[:, :, 0, :]
    o_d = mla_attention(q_nope, q_rope, k_nope, k_rope, v_d)
    o = jnp.concatenate([o_c.reshape(b, s, W_SB), o_d.reshape(b, s, W_MLA)], axis=-1)
    return o @ w_out

def squared_relu_mlp(h, w_up, w_down):
    return jnp.square(jax.nn.relu(h @ w_up)) @ w_down

def second_inputs(seed: int = 0) -> dict:
    key = jax.random.key(seed)
    ks = jax.random.split(key, 20)
    nrm = lambda k, shape, fan_in: jax.random.normal(k, shape, jnp.float32) * fan_in ** -0.5
    gain = lambda k, shape: 1.0 + 0.05 * jax.random.normal(k, shape, jnp.float32)
    x = jax.random.normal(ks[0], (BATCH, SEQ, D_MODEL), jnp.float32)
    offset = jax.random.randint(ks[1], (BATCH, 1), 0, 100000, dtype=jnp.int32)
    positions = offset + jnp.arange(SEQ, dtype=jnp.int32)[None, :]
    return {
        "x": x,
        "positions": positions,
        "norm_mix": gain(ks[2], (DEPTH_2, D_MODEL)),
        "norm_mlp": gain(ks[3], (DEPTH_2, D_MODEL)),
        "norm_final": gain(ks[4], (D_MODEL,)),
        "w_in_ab": nrm(ks[5], (N_EVEN, D_MODEL, IN_AB), D_MODEL),
        "b_forget": FORGET_BIAS + 0.5 * jax.random.normal(ks[6], (N_EVEN, H_FOX), jnp.float32),
        "rel_bias": 0.2 * jax.random.normal(ks[7], (N_EVEN, H_CHK, N_REL), jnp.float32),
        "w_out_ab": nrm(ks[8], (N_EVEN, MIX_AB, D_MODEL), MIX_AB),
        "w_in_cd": nrm(ks[9], (N_ODD, D_MODEL, IN_CD), D_MODEL),
        "q_norm": gain(ks[10], (N_ODD, Q_LORA)),
        "kv_norm": gain(ks[11], (N_ODD, KV_LORA)),
        "w_uq": nrm(ks[12], (N_ODD, Q_LORA, H_MLA * (NOPE_DIM + ROPE_DIM)), Q_LORA),
        "w_ukv": nrm(ks[13], (N_ODD, KV_LORA, H_MLA * (NOPE_DIM + V_DIM)), KV_LORA),
        "w_out_cd": nrm(ks[14], (N_ODD, MIX_CD, D_MODEL), MIX_CD),
        "w_up": nrm(ks[15], (DEPTH_2, D_MODEL, D_FF_2), D_MODEL),
        "w_down": nrm(ks[16], (DEPTH_2, D_FF_2, D_MODEL), D_FF_2),
    }

def second_block(x, positions, norm_mix, norm_mlp, norm_final, w_in_ab, b_forget, rel_bias, w_out_ab,
              w_in_cd, q_norm, kv_norm, w_uq, w_ukv, w_out_cd, w_up, w_down):
    for layer in range(DEPTH_2):
        h = rmsnorm(x, norm_mix[layer])
        if layer % 2 == 0:
            e = layer // 2
            x = x + even_mixer(h, w_in_ab[e], b_forget[e], rel_bias[e], w_out_ab[e])
        else:
            o = layer // 2
            x = x + odd_mixer(h, positions, w_in_cd[o], q_norm[o], kv_norm[o], w_uq[o], w_ukv[o], w_out_cd[o])
        x = x + squared_relu_mlp(rmsnorm(x, norm_mlp[layer]), w_up[layer], w_down[layer])
    return rmsnorm(x, norm_final)


def setup_inputs(seed=0):
    out = dict(first_inputs(seed))
    for name, value in second_inputs(seed + 1).items():
        if name != "x":
            out[name + "_2"] = value
    return out


def reference(
    x, rel_bias, hgrn_lb, ln_mix_g, w_in, q_norm_g, k_norm_g, hgrn_norm_g, conv_w, w_up_attn,
    w_up_hgrn, w_up_conv, w_out, ln_mlp_g, w_mlp_up, w_mlp_down, positions_2, norm_mix_2,
    norm_mlp_2, norm_final_2, w_in_ab_2, b_forget_2, rel_bias_2, w_out_ab_2, w_in_cd_2,
    q_norm_2, kv_norm_2, w_uq_2, w_ukv_2, w_out_cd_2, w_up_2, w_down_2,
):
    x = first_block(
        x, rel_bias, hgrn_lb, ln_mix_g, w_in, q_norm_g, k_norm_g, hgrn_norm_g, conv_w,
        w_up_attn, w_up_hgrn, w_up_conv, w_out, ln_mlp_g, w_mlp_up, w_mlp_down,
    )
    return second_block(
        x, positions_2, norm_mix_2, norm_mlp_2, norm_final_2, w_in_ab_2, b_forget_2, rel_bias_2,
        w_out_ab_2, w_in_cd_2, q_norm_2, kv_norm_2, w_uq_2, w_ukv_2, w_out_cd_2, w_up_2,
        w_down_2,
    )


_drawn_inputs = setup_inputs


def setup_inputs(seed=0):
    import zlib

    import numpy as np

    out = dict(_drawn_inputs(seed))
    spreads = {}
    factors = {'q_norm_g': 8.0,
     'k_norm_g': 8.0,
     'hgrn_norm_g': 8.0,
     'ln_mlp_g': 3.003,
     'norm_mix_2': 2.672,
     'rel_bias_2': 4.986,
     'q_norm_2': 8.0,
     'kv_norm_2': 7.033}
    for name, (base, spread) in spreads.items():
        noise = np.random.default_rng([zlib.crc32(name.encode()), seed]).standard_normal(out[name].shape)
        drawn = base * np.exp(spread * noise) if base else spread * noise
        out[name] = __import__('jax').numpy.asarray(drawn.astype(out[name].dtype))
    for name, factor in factors.items():
        out[name] = (out[name] * factor).astype(out[name].dtype)
    return out
```

```python
from contextlib import ExitStack

import concourse.bass as bass
import numpy as np
from concourse import mybir

F32 = mybir.dt.float32
F32R = mybir.dt.float32r
I32 = mybir.dt.int32
ALU = mybir.AluOpType
ACT = mybir.ActivationFunctionType
AX = mybir.AxisListType

P = 128
S = 256
TT = S // P
D = 1024
KT = D // P
UNIT = 1024
RAW = 4
RING = 8
LEAD = 6
EPS = 1e-6
NEG = -1e30
TAKEN = -3e38
FF = 4096
GROUP = 512
NG = FF // GROUP
HB = 32
NHB = S // HB


def plan():
    jobs, u, pair = {}, 0, 0

    def add(name, kind, cols, nkt):
        nonlocal u, pair
        kpu = KT if kind == "F" else min(nkt, UNIT // cols)
        n = cols // P if kind == "F" else -(-nkt // kpu)
        jobs[name] = dict(kind=kind, cols=cols, nkt=nkt, kpu=kpu, u0=u, n=n, pair=pair % 2)
        u += n
        pair += 1

    def mlp(i):
        nonlocal u, pair
        jobs[f"mlp{i}"] = dict(kind="M", u0=u, n=NG * 8, pair=pair % 2)
        u += NG * 8
        pair += NG

    for name, kind, cols in (("aq", "T", 512), ("akv", "T", 260), ("iqk", "F", 384), ("hf", "F", 512),
                             ("hq", "F", 512), ("hi", "T", 512), ("cc", "F", 512), ("ch", "F", 512),
                             ("cb", "F", 512), ("hg", "T", 512)):
        add(name, kind, cols, KT)
    for b in (2, 1, 0):
        add(f"g{b}0", "T", 512, KT)
        add(f"g{b}1", "T", 512, KT)
        add(f"u{b}0", "T", 512, 4)
        add(f"u{b}1", "T", 512, 4)
    add("wo0", "T", 512, KT)
    add("wo1", "T", 512, KT)
    mlp(0)
    for name, kind, cols in (("fa", "T", 8), ("fq", "F", 512), ("fk", "F", 512), ("fv", "T", 512),
                             ("bq", "F", 512), ("bk", "F", 512), ("bv", "T", 512)):
        add(name, kind, cols, KT)
    jobs["woa"] = dict(kind="O", u0=u, n=8, pair=pair % 2)
    u += 8
    pair += 2
    mlp(1)
    for name, kind, cols, nkt in (("cq", "T", 384, KT), ("ckv", "T", 288, KT), ("sq", "F", 512, KT),
                                  ("sk", "F", 512, KT), ("uq0", "T", 512, 3), ("uq1", "T", 256, 3),
                                  ("kn", "T", 512, 2), ("vn", "T", 512, 2), ("sv", "T", 512, KT)):
        add(name, kind, cols, nkt)
    jobs["wob"] = dict(kind="O", u0=u, n=8, pair=pair % 2)
    u += 8
    pair += 2
    mlp(2)
    return jobs, u


JOBS, UNITS = plan()

C_ID, C_FLIP, C_TRI, C_ONE, C_NSUF, C_NONE, C_Z, C_CM, C_Z2, C_CK, C_ST, C_BD = (P * i for i in range(12))
C_OH = 12 * P
C_FREQ = C_OH + 384
C_BLK = C_FREQ + 16
N_CONST = C_BLK + 4
G_MIX, G_MLP, G_N2, G_M2 = 0, 8, 16, 32
G_Q, G_K, G_CONV, G_CQ, G_CKV, G_H, G_BF = 48, 49, 50, 62, 65, 67, 195
N_SMALL = 203

TURN = []
_rest = 2 * np.pi
for _ in range(4):
    _e = int(np.floor(np.log2(_rest))) - 7
    _part = float(np.floor(_rest / 2.0**_e) * 2.0**_e)
    TURN.append(_part)
    _rest -= _part
TURN.append(float(_rest))
MAGIC = 1.5 * 2.0**23
ARENA = 20240


def model(nc, stream, const, small, pos, relb, rb2, gfin, x_in, scratch, out):
    with ExitStack() as ctx:
        def sb(name, shape, dt=F32):
            return ctx.enter_context(nc.sbuf_tensor(name, shape, dt))

        sems = {}

        def sem(name):
            if name not in sems:
                sems[name] = ctx.enter_context(nc.semaphore(name))
            return sems[name]

        raw = sb("raw", [P, RAW, UNIT])
        whi = sb("whi", [P, RING, UNIT], F32R)
        wlo = sb("wlo", [P, RING, UNIT], F32R)
        x = sb("x", [P, TT, D])
        hT = [sb("hT_hi", [P, KT, S], F32R), sb("hT_lo", [P, KT, S], F32R)]
        Y = [sb("y_hi", [P, 2, 4, S], F32R), sb("y_lo", [P, 2, 4, S], F32R)]
        cst = sb("cst", [P, N_CONST])
        sml = sb("sml", [P, N_SMALL])
        bm = sb("bm", [P, 8, 3 * P])
        stat = sb("stat", [P, 256])
        posi = sb("posi", [P, TT], I32)
        arena = sb("arena", [P, ARENA])
        ps = ctx.enter_context(nc.psum_tensor("ps", [P, 8, 512], F32))
        W0, W1, W2, W3 = 4, 5, 6, 7

        at = [0]

        def area(n, start=None):
            if start is not None:
                at[0] = start
            v = arena[:, at[0]:at[0] + n]
            at[0] += n
            assert at[0] <= ARENA, at[0]
            return v

        def c3(ap, **k):
            return ap.rearrange("p (a b) -> p a b", **k)

        def cs(col, n=P):
            return cst[:, col:col + n]

        hz = c3(area(1024, 0), a=4)
        hqf = c3(area(1024), a=4)
        hin = c3(area(1024), a=TT)
        hE = area(1024)
        hW = area(1024)
        hF = area(1024)
        hX = area(1024)
        hS = c3(area(1024), a=8)
        i4 = c3(area(1024), a=TT)
        hA = c3(area(256), a=TT)
        hMask = area(256)
        ccT = c3(area(1024), a=4)
        chT = c3(area(1024), a=4)
        cbT = c3(area(1024), a=4)
        hgt = c3(area(1024), a=TT)
        gate = c3(area(2048), a=TT)
        qraw = c3(area(1024), a=TT)
        kvw = c3(area(520), a=TT)
        after_kvw = at[0]
        qTd = c3(area(1024), a=4)
        kTd = area(256)
        att = area(1536)
        Lb = c3(att[:, 0:512], a=2)
        Pb = c3(att[:, 512:1024], a=2)
        PTb = c3(att[:, 1024:1536], a=2)
        ATT_END = at[0]
        khT = c3(hz.rearrange("p a b -> p (a b)"), a=TT)
        ho = c3(hF, a=TT)
        up_e = cbT.rearrange("p a b -> p (a b)").rearrange("p (a b) -> p a b", a=TT)
        mixed = arena[:, 9 * 1024 + 512:9 * 1024 + 512 + 2048].rearrange("p (a b) -> p a b", a=TT)
        o_all = up_t = qTd.rearrange("p a b -> p (a b)").rearrange("p (a b) -> p a b", a=TT)
        cv_y = cbT
        t5_row = att[0:8, 0:384]
        iqk = c3(hX[:, 0:768], a=3)
        ir0 = c3(hE[:, 0:512], a=4)
        ir1 = c3(hW, a=4)
        isc = hF[:, 0:384]
        imask = hF[:, 384:768]
        Hank = gate.rearrange("p a b -> p (a b)").rearrange("p (a b) -> p a b", a=8)
        y_tok = qraw
        relu = c3(area(2048, 0), a=2)
        sqr = area(1024)
        gbc = arena[:, 5120:6144]
        a2 = 4096
        fq = c3(area(1024, a2), a=4)
        fk = c3(area(1024), a=4)
        fv = c3(area(1024), a=TT)
        bq = c3(area(1024), a=4)
        bk = c3(area(1024), a=4)
        bv = c3(area(1024), a=TT)
        y2 = c3(area(1024), a=TT)
        fa = c3(area(16), a=TT)
        assert at[0] < after_kvw
        bm2 = arena[:, 0:3072].rearrange("p (a b) -> p a b", a=8)
        Hank2 = arena[:, 3072 + 9216:3072 + 9216 + 2048].rearrange("p (a b) -> p a b", a=8)
        cqt = c3(area(768, a2), a=TT)
        ckt = c3(area(576), a=TT)
        sq = c3(area(1024), a=4)
        sk = c3(area(1024), a=4)
        sv = c3(area(1024), a=TT)
        qtk = c3(area(1536), a=TT)
        knt = c3(area(1024), a=TT)
        kfl = c3(area(1536), a=TT)
        vnt = c3(area(1024), a=TT)
        y3 = c3(area(1024), a=TT)
        rot = c3(area(64), a=TT)
        rtmp = area(512)
        sbt = c3(area(768), a=2)
        sbn = c3(area(768), a=2)
        assert at[0] < after_kvw, (at[0], after_kvw)
        qTm = c3(arena[:, 0:2048], a=8)
        kTm = c3(arena[:, 2048:4096], a=8)

        ss = stat[:, 0:2]
        rs = stat[:, 2:4]
        nt = stat[:, 4:6]
        st20 = stat[:, 8:28]
        rs20 = stat[:, 28:48]
        nt20 = stat[:, 48:68]
        mx = stat[:, 68:84]
        nmx = stat[:, 84:100]
        sums = stat[:, 100:116]
        rsum = stat[:, 116:132]
        top8 = stat[:, 132:140]
        wi = stat[:, 140:148].rearrange("p (a b) -> p a b", a=TT)
        g8 = stat[:, 148:149]
        cnq = stat[:, 150:166]
        hm = stat[:, 168:200]
        hdT = stat[:, 200:232]
        bias1 = stat[:, 255:256]

        block = ctx.enter_context(nc.Block())

        def last_unit(name):
            return JOBS[name]["u0"] + JOBS[name]["n"] - 1

        emptied = [n for n in JOBS if JOBS[n]["kind"] in "TF" and not n.startswith("wo")]
        count, evac_no = 0, {}
        for n in JOBS:
            if n in emptied:
                evac_no[n] = count
                count += 1
            elif JOBS[n]["kind"] == "M":
                evac_no[n] = count
                count += NG
        NORMS = ("n_mix", "n_mlp0", "n_ab", "n_mlp1", "n_cd", "n_mlp2")
        GAIN = (G_MIX, G_MLP, G_N2, G_M2, G_N2 + 8, G_M2 + 8)

        @block.sync
        def _(sp):
            sp.dma_start(x[:], x_in.rearrange("(t p) d -> p t d", p=P)).then_inc(sem("x_in"), 16)
            sp.dma_start(cst[:], const).then_inc(sem("c_in"), 16)
            sp.dma_start(sml[:], small).then_inc(sem("c_in"), 16)

            def load(u):
                if u >= RAW:
                    sp.wait_ge(sem("lo_done"), u - RAW + 1)
                sp.dma_start(raw[:, u % RAW, :], stream[u]).then_inc(sem(f"ld{u % RAW}"), 16)

            for u in range(RAW):
                load(u)
            sp.dma_start(stat[0:32, 232:240], relb).then_inc(sem("relb_in"), 16)
            sp.dma_start(posi[:], pos).then_inc(sem("p_in"), 16)
            for u in range(RAW, JOBS["mlp0"]["u0"] + 60):
                load(u)
            sp.dma_start(Hank2, bass.AP(rb2.tensor, 0, [[1, P], [400, 8], [1, S]])).then_inc(sem("hank"), 16)
            for u in range(JOBS["mlp0"]["u0"] + 60, UNITS):
                load(u)
                if u == JOBS["mlp2"]["u0"] + 30:
                    sp.dma_start(gbc, bass.AP(gfin.tensor, 0, [[0, P], [1, D]])).then_inc(sem("g_in"), 16)
            for t in range(TT):
                sp.wait_ge(sem("y_out"), t + 1)
                sp.dma_start(out.rearrange("(t p) d -> p t d", p=P)[:, t, :], x[:, t, :]).then_inc(sem("stored"), 16)
            sp.wait_ge(sem("stored"), 16 * TT)

        @block.tensor
        def _(pe):
            def three(o, a, b, start, stop):
                pe.matmul(o, a[0], b[0], start=start, stop=False)
                pe.matmul(o, a[0], b[1], start=False, stop=False)
                return pe.matmul(o, a[1], b[0], start=False, stop=stop)

            def wsl(u, a, b):
                return whi[:, u % RING, a:b], wlo[:, u % RING, a:b]

            order = [n for n in JOBS]
            pairs = []
            for n in order:
                k = JOBS[n]["kind"]
                if k in "TF":
                    pairs.append((n, evac_no[n] if n in emptied else None))
                elif k == "M":
                    pairs += [((n, g), evac_no[n] + g) for g in range(NG)]
                else:
                    pairs += [((n, 0), None), ((n, 1), None)]
            idx = {n: i for i, (n, _) in enumerate(pairs)}

            def pair_free(key):
                i = idx[key]
                if i >= 2 and pairs[i - 2][1] is not None:
                    pe.wait_ge(sem("evac"), pairs[i - 2][1] + 1)
                return 2 * (i % 2)

            def unit(name, k, X):
                j = JOBS[name]
                u = j["u0"] + k
                if k == 0:
                    j["bank"] = pair_free(name)
                pe.wait_ge(sem("lo_done"), u + 1)
                b = j["bank"]
                if j["kind"] == "F":
                    o = ps[:, b + k // 2, (k % 2) * S:(k % 2 + 1) * S]
                    for kt in range(KT):
                        m = three(o, wsl(u, kt * P, (kt + 1) * P), X(kt), kt == 0, kt == KT - 1)
                else:
                    w = j["cols"]
                    kts = range(k * j["kpu"], min((k + 1) * j["kpu"], j["nkt"]))
                    for t in range(TT):
                        for kt in kts:
                            c = (kt - kts[0]) * w
                            m = three(ps[:, b + t, 0:w], X(kt, t), wsl(u, c, c + w), kt == 0, kt == j["nkt"] - 1)
                m.then_inc(sem("used"), 1)

            def h_all(kt, t=None):
                c = slice(0, S) if t is None else slice(t * P, (t + 1) * P)
                return hT[0][:, kt, c], hT[1][:, kt, c]

            def y_of(slot):
                def f(kt, t):
                    c = slice(t * P, (t + 1) * P)
                    return Y[0][:, slot, kt, c], Y[1][:, slot, kt, c]
                return f

            def tr(o, i, n=P):
                return pe.transpose(o, i, cst[0:n, C_ID:C_ID + n])

            def norm(i):
                for t in range(TT):
                    pe.wait_ge(sem("n_x"), TT * i + t + 1)
                for b in range(4):
                    for k in (2 * b, 2 * b + 1):
                        for t in range(TT):
                            m = tr(ps[:, W0 + b, (k % 2) * S + t * P:(k % 2) * S + (t + 1) * P],
                                   x_n[:, t, k * P:(k + 1) * P])
                    m.then_inc(sem("n_tr"), 1)
                pe.wait_ge(sem("n_lo"), 4 * (i + 1))

            x_n = arena[:, 0:2048].rearrange("p (a b) -> p a b", a=TT)

            def att_logits(a, n, q, k):
                t, h = divmod(n, 8)
                N = 16 * a + n
                if n >= 2:
                    pe.wait_ge(sem("att_nmx"), N - 1)
                w = P * (t + 1)
                pe.matmul(ps[:, W0 + n % 2, 0:w], q(h, t), k(h, w), start=True, stop=True).then_inc(sem("att_qk"), 1)

            def att_turn(a, n):
                t = n // 8
                N = 16 * a + n
                pe.wait_ge(sem("att_exp"), N + 1)
                if n >= 1:
                    pe.wait_ge(sem("att_ptc"), N)
                for kt in range(t + 1):
                    m = tr(ps[:, W2, kt * P:(kt + 1) * P], Pb[:, n % 2, kt * P:(kt + 1) * P])
                m.then_inc(sem("att_tr"), 1)

            def att_values(a, n, v):
                t, h = divmod(n, 8)
                N = 16 * a + n
                pe.wait_ge(sem("att_ptc"), N + 1)
                if h == 0 and t == 1:
                    pe.wait_ge(sem("att_on"), TT * a + 1)
                for kt in range(t + 1):
                    m = pe.matmul(ps[:, W3, h * 64:(h + 1) * 64], PTb[:, n % 2, kt * P:(kt + 1) * P], v(h, kt),
                                  start=kt == 0, stop=kt == t)
                m.then_inc(sem("att_pv"), 1)

            def att_step(a, n, q, k, v):
                if n == 0:
                    att_logits(a, 0, q, k)
                if n < 15:
                    att_logits(a, n + 1, q, k)
                att_turn(a, n)
                if n >= 1:
                    att_values(a, n - 1, v)
                if n == 15:
                    att_values(a, 15, v)

            def tok_to_feat(src):
                for b in range(2):
                    for k in (2 * b, 2 * b + 1):
                        for t in range(TT):
                            m = tr(ps[:, W0 + b, (k % 2) * S + t * P:(k % 2) * S + (t + 1) * P],
                                   src[:, t, k * P:(k + 1) * P])
                m.then_inc(sem("y_tr"), 1)

            pe.wait_ge(sem("c_in"), 32)
            pe.wait_ge(sem("relb_in"), 16)
            pe.matmul(ps[0:8, 0, 0:384], stat[0:32, 232:240], cst[0:32, C_OH:C_OH + 384],
                      start=True, stop=True).then_inc(sem("t5_ps"), 1)
            norm(0)
            pe.wait_ge(sem("t5_row"), 1)

            def dsa_q(h, t):
                g = slice(64 * (h // 4), 64 * (h // 4) + 64)
                return qTd[g, h % 4, t * P:(t + 1) * P]

            def dsa_k(h, w):
                return kTd[64 * (h // 4):64 * (h // 4) + 64, 0:w]

            def dsa_v(h, kt):
                return kvw[:, kt, P + 64 * (h // 4):P + 64 * (h // 4) + 64]

            def hgrn(hd, stage):
                if stage == 0:
                    pe.wait_ge(sem("hg_f"), 1)
                    for t in range(TT):
                        c = slice(t * P, (t + 1) * P)
                        m = pe.matmul(ps[:, W0, c], c3(hW, a=4)[:, hd, c], c3(hF, a=4)[:, hd, c],
                                      start=True, stop=True)
                    m.then_inc(sem("hg_a"), 1)
                    for t in range(TT):
                        c = slice(t * P, (t + 1) * P)
                        m = tr(ps[:, W1, c], c3(hX, a=4)[:, hd, c])
                    m.then_inc(sem("hg_kt"), 1)
                elif stage == 1:
                    pe.wait_ge(sem("hg_i4"), hd + 1)
                    pe.wait_ge(sem("hg_ktc"), hd + 1)
                    for t in range(TT):
                        m = pe.matmul(ps[:, W2 if t == 0 else W1, :], khT[:, t, hd * P:(hd + 1) * P], i4[:, t, :],
                                      start=True, stop=True)
                        m.then_inc(sem("hg_u"), 1)
                else:
                    pe.wait_ge(sem("hg_am"), hd + 1)
                    if hd >= 1:
                        pe.wait_ge(sem("hg_oc"), hd)
                    for t in range(TT):
                        o = ps[:, W3, t * P:(t + 1) * P]
                        m = pe.matmul(o, hA[:, t, :], hin[:, t, hd * P:(hd + 1) * P], start=True, stop=True)
                        for b in range(P // HB):
                            n = t * (P // HB) + b
                            if n == 0:
                                continue
                            pe.wait_ge(sem("hg_s"), 7 * hd + n)
                            m = pe.matmul(ps[b * HB:(b + 1) * HB, W3, t * P:(t + 1) * P],
                                          c3(hE, a=4)[:, hd, n * HB:(n + 1) * HB], hS[:, n, :],
                                          start=False, stop=True, skip_group_check=True)
                    m.then_inc(sem("hg_o"), 1)

            seq = []
            for name in ("aq", "akv", "iqk", "hf", "hq", "hi", "cc", "ch", "cb", "hg"):
                seq += [(name, k, h_all) for k in range(JOBS[name]["n"])]
            for b, slot in ((2, 0), (1, 1), (0, 0)):
                for nm, X in ((f"g{b}0", h_all), (f"g{b}1", h_all), (f"u{b}0", y_of(slot)), (f"u{b}1", y_of(slot))):
                    seq += [(nm, k, X) for k in range(JOBS[nm]["n"])]
            for u, (name, k, X) in enumerate(seq):
                if name in ("u20", "u10", "u00") and k == 0:
                    pe.wait_ge(sem("y_lo"), {"u20": 1, "u10": 3, "u00": 3}[name])
                unit(name, k, X)
                if u == 9:
                    pe.wait_ge(sem("qk_n"), 1)
                    for t in range(TT):
                        m = tr(ps[:, W0, t * P:(t + 1) * P], kvw[:, t, 0:P])
                    for j in range(4):
                        for t in range(TT):
                            m = tr(ps[:, W1 + j // 2, (j % 2) * S + t * P:(j % 2) * S + (t + 1) * P],
                                   qraw[:, t, j * P:(j + 1) * P])
                    m.then_inc(sem("qk_tr"), 1)
                if u == 10:
                    pe.wait_ge(sem("evac"), evac_no["iqk"] + 1)
                    pe.wait_ge(sem("qk_T"), 1)
                    for t in range(TT):
                        w = P * (t + 1)
                        for h in range(4):
                            g = slice(64 * (h % 2), 64 * (h % 2) + 64)
                            o = ps[:, (W2 if t == 0 else W0) + h % 2, (h // 2) * w:(h // 2 + 1) * w]
                            m = pe.matmul(o, iqk[g, h // 2, t * P:(t + 1) * P], iqk[g, 2, 0:w], start=True, stop=True)
                        m.then_inc(sem("idx"), 1)
                if u == 22:
                    pe.wait_ge(sem("hank"), 16)
                    pe.wait_ge(sem("idx_r"), 2)
                    for g in range(4):
                        pe.matmul(ps[:, W0 + g, :], cs(C_FLIP), Hank[:, 2 * g:2 * g + 2, :],
                                  start=True, stop=True).then_inc(sem("bm_ps"), 1)
                if 24 <= u < 40:
                    if u == 24:
                        pe.wait_ge(sem("bm_ok"), 1)
                    att_step(0, u - 24, dsa_q, dsa_k, dsa_v)
                if 42 <= u < 54:
                    if u == 42:
                        pe.wait_ge(sem("att_on"), 2)
                    hgrn((u - 42) // 3, (u - 42) % 3)
                if u == 54:
                    tok_to_feat(y_tok)
                if u == 57:
                    pe.wait_ge(sem("hg_y"), 1)
                    pe.wait_ge(sem("y_lo"), 2)
                    tok_to_feat(ho)
            pe.wait_ge(sem("mixed"), 6)
            for b in range(4):
                for k in (2 * b, 2 * b + 1):
                    for t in range(TT):
                        m = tr(ps[:, W0 + b, (k % 2) * S + t * P:(k % 2) * S + (t + 1) * P],
                               mixed[:, t, k * P:(k + 1) * P])
                m.then_inc(sem("mx_tr"), 1)
            pe.wait_ge(sem("mx_lo"), 4)
            for name in ("wo0", "wo1"):
                for k in range(4):
                    unit(name, k, h_all)

            def mlp(i):
                base = JOBS[f"mlp{i}"]["u0"]

                def up(g, u):
                    b = pair_free((f"mlp{i}", g))
                    for k in range(4):
                        pe.wait_ge(sem("lo_done"), u + k + 1)
                        o = ps[:, b + k // 2, (k % 2) * S:(k % 2 + 1) * S]
                        for kt in range(KT):
                            m = three(o, wsl(u + k, kt * P, (kt + 1) * P), h_all(kt), kt == 0, kt == KT - 1)
                        m.then_inc(sem("used"), 1)

                def down(g, u):
                    pe.wait_ge(sem("m_lo"), NG * i + g + 1)
                    for k in range(4):
                        pe.wait_ge(sem("lo_done"), u + k + 1)
                        half = k // 2
                        for t in range(TT):
                            for q in range(2):
                                kt = 2 * (k % 2) + q
                                m = three(ps[:, W0 + TT * half + t, :], y_of(g % 2)(kt, t),
                                          wsl(u + k, q * 512, (q + 1) * 512),
                                          g == 0 and kt == 0, g == NG - 1 and kt == 3)
                        m.then_inc(sem("used"), 1)

                up(0, base)
                for g in range(1, NG):
                    up(g, base + 8 * g - 4)
                    down(g - 1, base + 8 * g)
                down(NG - 1, base + 8 * NG - 4)

            def out_unit(name, k):
                j = JOBS[name]
                u = j["u0"] + k
                kh, half, q = k // 4, (k // 2) % 2, k % 2
                if k in (0, 2):
                    j[half] = pair_free((name, half))
                pe.wait_ge(sem("lo_done"), u + 1)
                for t in range(TT):
                    for kk in range(2):
                        kt = 2 * q + kk
                        m = three(ps[:, j[half] + t, :], y_of(kh)(kt, t), wsl(u, kk * 512, (kk + 1) * 512),
                                  kh == 0 and kt == 0, kh == 1 and kt == 3)
                m.then_inc(sem("used"), 1)

            norm(1)
            mlp(0)

            norm(2)

            def mh_q(T):
                return lambda h, t: T[64 * (h % 2):64 * (h % 2) + 64, h // 2, t * P:(t + 1) * P]

            def mh_k(T):
                return lambda h, w: T[64 * (h % 2):64 * (h % 2) + 64, h // 2, 0:w]

            def mh_v(T):
                return lambda h, kt: T[:, kt, 64 * h:64 * h + 64]

            seq = [(n, k) for n in ("fa", "fq", "fk", "fv", "bq", "bk", "bv") for k in range(JOBS[n]["n"])]
            done = 0
            for u, (name, k) in enumerate(seq):
                unit(name, k, h_all)
                if u == 1:
                    pe.wait_ge(sem("fx_n"), 1)
                    pe.matmul(ps[:, W0, 0:8], cs(C_TRI), fa[:, 0, :], start=True, stop=True)
                    pe.matmul(ps[:, W0, 8:16], cs(C_ONE), fa[:, 0, :], start=True, stop=False)
                    pe.matmul(ps[:, W0, 8:16], cs(C_TRI), fa[:, 1, :], start=False, stop=True).then_inc(sem("fx_cn"), 1)
                if 3 <= u < 11:
                    h = u - 3
                    b = W1 + h % 2
                    if h >= 2:
                        pe.wait_ge(sem("fx_bm"), h - 1)
                    pe.matmul(ps[:, b, 0:S], fa[:, 0, h:h + 1].to_broadcast([P, P]), cst[:, C_TRI:C_TRI + S],
                              start=True, stop=True)
                    pe.matmul(ps[:, b, P:S], fa[:, 1, h:h + 1].to_broadcast([P, P]), cs(C_TRI),
                              start=False, stop=True, skip_group_check=True).then_inc(sem("fx_bc"), 1)
                if u == 11:
                    pe.wait_ge(sem("fx_bm"), 8)
                    pe.wait_ge(sem("hank"), 32)
                    for g in range(4):
                        pe.matmul(ps[:, W0 + g, :], cs(C_FLIP), Hank2[:, 2 * g:2 * g + 2, :],
                                  start=True, stop=True).then_inc(sem("bm_ps"), 1)
                if u == 13:
                    pe.wait_ge(sem("bm_ok"), 2)
                    pe.wait_ge(sem("evac"), evac_no["fv"] + 1)
                if 13 <= u < 25:
                    for n in range((u - 13) * 4 // 3, (u - 12) * 4 // 3):
                        att_step(1, n, mh_q(fq), mh_k(fk), mh_v(fv))
            pe.wait_ge(sem("att_on"), 4)
            tok_to_feat(y2)
            pe.wait_ge(sem("evac"), evac_no["bv"] + 1)
            pe.wait_ge(sem("y_lo"), 4)
            for n in range(16):
                att_step(2, n, mh_q(bq), mh_k(bk), mh_v(bv))
                if n % 4 == 3:
                    out_unit("woa", n // 4)
            pe.wait_ge(sem("att_on"), 6)
            tok_to_feat(y2)
            pe.wait_ge(sem("y_lo"), 5)
            for k in range(4, 8):
                out_unit("woa", k)
            norm(3)
            mlp(1)

            norm(4)

            def lat(slot, n):
                def f(kt, t):
                    c = slice(t * P, (t + 1) * P)
                    return Y[0][:, slot, kt, c], Y[1][:, slot, kt, c]
                return f

            def sb_scores(h):
                g = slice(64 * (h % 2), 64 * (h % 2) + 64)
                b = W0 + h % 2
                if h >= 2:
                    pe.wait_ge(sem("sb_a"), h - 1)
                pe.matmul(ps[:, b, 0:S], sk[g, h // 2, 0:P], sq[g, h // 2, :], start=True, stop=True)
                pe.matmul(ps[:, b, S:S + P], sk[g, h // 2, P:S], sq[g, h // 2, P:S], start=False, stop=True,
                          skip_group_check=True)
                for c in (0, S):
                    m = pe.matmul(ps[:, b, c:c + P], cs(C_ID), cs(C_ST), start=False, stop=True, skip_group_check=True)
                m.then_inc(sem("sb_z"), 1)

            def sb_sums(h):
                b = W0 + h % 2
                n = sbn[:, h % 2, :]
                pe.wait_ge(sem("sb_n"), h + 1)
                pe.matmul(ps[:, b, 0:S], cs(C_NSUF), n[:, 0:S], start=False, stop=True, skip_group_check=True)
                pe.matmul(ps[:, b, P:S], cs(C_NONE), n[:, S:S + P], start=False, stop=True, skip_group_check=True)
                pe.matmul(ps[:, b, S:S + P], cs(C_NSUF), n[:, S:S + P], start=False, stop=True,
                          skip_group_check=True).then_inc(sem("sb_r"), 1)

            def sb_values(h):
                g = slice(64 * (h % 2), 64 * (h % 2) + 64)
                b = W2 + (h // 2) % 2
                a = sbt[:, h % 2, :]
                pe.wait_ge(sem("sb_a"), h + 1)
                if h >= 4 and h % 2 == 0:
                    pe.wait_ge(sem("sb_lo"), h // 2 - 1)
                pe.matmul(ps[g, b, 0:S], sv[:, 0, 64 * h:64 * h + 64], a[:, 0:S], start=True, stop=True)
                m = pe.matmul(ps[g, b, P:S], sv[:, 1, 64 * h:64 * h + 64], a[:, S:S + P], start=False, stop=True,
                              skip_group_check=True)
                m.then_inc(sem("sb_v"), 1)

            def mla_turn(src, c0):
                for h4 in range(2):
                    if c0 + h4 >= 1:
                        pe.wait_ge(sem("ml_T"), c0 + h4)
                    for h in range(4 * h4, 4 * h4 + 4):
                        for t in range(TT):
                            o = ps[0:96, W2 + (h % 4) // 2, (h % 2) * S + t * P:(h % 2) * S + (t + 1) * P]
                            m = pe.transpose(o, src[:, t, 96 * h:96 * h + 96], cs(C_ID))
                    m.then_inc(sem("ml_tr"), 1)

            seq = [(n, k) for n in ("cq", "ckv", "sq", "sk", "uq0", "uq1", "kn", "vn", "sv")
                   for k in range(JOBS[n]["n"])]
            for u, (name, k) in enumerate(seq):
                if name == "uq0" and k == 0:
                    pe.wait_ge(sem("la_lo"), 1)
                X = {"uq0": lat(0, 3), "uq1": lat(0, 3), "kn": lat(1, 2), "vn": lat(1, 2)}.get(name, h_all)
                unit(name, k, X)
                if u == 9:
                    pe.wait_ge(sem("la_n"), 1)
                    for kt in range(3):
                        for t in range(TT):
                            m = tr(ps[:, W0 + kt // 2, (kt % 2) * S + t * P:(kt % 2) * S + (t + 1) * P],
                                   cqt[:, t, kt * P:(kt + 1) * P])
                    for kt in range(2):
                        for t in range(TT):
                            m = tr(ps[:, W2, kt * S + t * P:kt * S + (t + 1) * P], ckt[:, t, kt * P:(kt + 1) * P])
                    m.then_inc(sem("la_tr"), 1)
            pe.wait_ge(sem("evac"), evac_no["sv"] + 1)
            sb_scores(0)
            for h in range(8):
                if h < 7:
                    sb_scores(h + 1)
                sb_sums(h)
                sb_values(h)
            pe.wait_ge(sem("sb_lo"), 4)
            pe.wait_ge(sem("ro_q"), 1)
            mla_turn(qtk, 0)
            pe.wait_ge(sem("ro_k"), 1)
            mla_turn(kfl, 2)
            pe.wait_ge(sem("ml_T"), 4)
            for n in range(16):
                att_step(3, n, lambda h, t: qTm[0:96, h, t * P:(t + 1) * P], lambda h, w: kTm[0:96, h, 0:w], mh_v(vnt))
                if n % 4 == 3:
                    out_unit("wob", n // 4)
            pe.wait_ge(sem("att_on"), 8)
            tok_to_feat(y3)
            pe.wait_ge(sem("y_lo"), 6)
            for k in range(4, 8):
                out_unit("wob", k)
            norm(5)
            mlp(2)

        @block.scalar
        def _(act):
            link_no = [0]

            def link(i):
                link_no[0] += 1
                i.then_inc(sem("act_link"), 1)
                act.wait_ge(sem("act_link"), link_no[0])

            def hi(u):
                if u >= UNITS:
                    return
                act.wait_ge(sem(f"ld{u % RAW}"), 16 * (u // RAW + 1))
                if u >= RING:
                    act.wait_ge(sem("used"), u - RING + 1)
                act.activation(whi[:, u % RING, :], raw[:, u % RAW, :], ACT.Copy).then_inc(sem("hi_done"), 1)

            pair_no = [0]

            def evac(name, dst, func=ACT.Copy, scale=1.0, wait=None):
                j = JOBS[name]
                b = 2 * pair_of[name]
                act.wait_ge(sem("used"), last_unit(name) + 1)
                for s, v in wait or ():
                    act.wait_ge(sem(s), v)
                if j["kind"] == "F":
                    n = j["cols"] // P
                    src = ps[:, b:b + 2, :].rearrange("p a (b c) -> p (a b) c", b=2)[:, 0:n, :]
                else:
                    src = ps[:, b:b + 2, 0:j["cols"]]
                act.activation(dst, src, func, scale=scale).then_inc(sem("evac"), 1)

            pair_of, c = {}, 0
            for n in JOBS:
                pair_of[n] = c % 2
                c += {"M": NG, "O": 2}.get(JOBS[n]["kind"], 1)

            def norm(i):
                for t in range(TT):
                    act.wait_ge(sem("x_ok" if i else "x_in"), TT * (i - 1) + t + 1 if i else 16)
                    act.activation(arena[:, 2048 + t * 1024:3072 + t * 1024], x[:, t, :], ACT.Square,
                                   accum_out=ss[:, t:t + 1]).then_inc(sem("n_ss"), 1)
                rsqrt(rs, nt, "n_v", i + 1, "n_r")
                if i == len(NORMS):
                    return
                for b in range(4):
                    act.wait_ge(sem("n_tr"), 4 * i + b + 1)
                    for k in (2 * b, 2 * b + 1):
                        m = act.activation(hT[0][:, k, :], ps[:, W0 + b, (k % 2) * S:(k % 2 + 1) * S], ACT.Copy,
                                           scale=sml[:, GAIN[i] + k:GAIN[i] + k + 1])
                    m.then_inc(sem("n_hi"), 1)

            def rsqrt(r, v, ready, count, signal):
                act.wait_ge(sem(ready), count)
                link(act.activation(r, v, ACT.Ln))
                act.activation(r, r, ACT.Exp, scale=-0.5).then_inc(sem(signal), 1)

            def att_step(a, n):
                def exps(n):
                    N = 16 * a + n
                    w = P * (n // 8 + 1)
                    act.wait_ge(sem("att_nmx"), N + 1)
                    if n >= 2:
                        act.wait_ge(sem("att_tr"), N - 1)
                    act.activation(Pb[:, n % 2, 0:w], Lb[:, n % 2, 0:w], ACT.Exp, bias=nmx[:, n:n + 1],
                                   accum_out=sums[:, n:n + 1]).then_inc(sem("att_exp"), 1)

                def copy(n):
                    N = 16 * a + n
                    w = P * (n // 8 + 1)
                    act.wait_ge(sem("att_tr"), N + 1)
                    if n >= 2:
                        act.wait_ge(sem("att_pv"), N - 1)
                    act.activation(PTb[:, n % 2, 0:w], ps[:, W2, 0:w], ACT.Copy).then_inc(sem("att_ptc"), 1)

                exps(n)
                if n >= 1:
                    copy(n - 1)
                if n == 15:
                    copy(15)

            def y_hi(no, slot):
                act.wait_ge(sem("y_tr"), no + 1)
                for b in range(2):
                    m = act.activation(Y[0][:, slot, 2 * b:2 * b + 2, :], ps[:, W0 + b, :], ACT.Copy)
                m.then_inc(sem("y_hi"), 1)

            act.preload_act_table_set("natural_log_exp_and_others")
            for u in range(RAW):
                hi(u)
            act.wait_ge(sem("t5_ps"), 1)
            act.activation(t5_row, ps[0:8, 0, 0:384], ACT.Copy).then_inc(sem("t5_row"), 1)
            act.wait_ge(sem("t5_row"), 1)
            act.dma_start(scratch[:, 0:384], t5_row).then_inc(sem("t5_out"), 16)
            for u in range(RAW, LEAD):
                hi(u)
            norm(0)
            act.wait_ge(sem("t5_out"), 16)
            act.dma_start(Hank, bass.AP(scratch.tensor, 0, [[1, P], [400, 8], [1, S]])).then_inc(sem("hank"), 16)
            L1 = {
                "aq": (qraw, ACT.Copy, 1.0, ()), "akv": (kvw, ACT.Copy, 1.0, ()), "iqk": (iqk, ACT.Copy, 1.0, ()),
                "hf": (hz, ACT.Copy, 1.0, ()), "hq": (hqf, ACT.Copy, 1.0, ()),
                "hi": (hin, ACT.Copy, 1.0, ()), "cc": (ccT, ACT.Copy, 1.0, ()), "ch": (chT, ACT.Copy, 1.0, ()),
                "cb": (cbT, ACT.Copy, 1.0, ()), "hg": (hgt, ACT.Copy, 1.0, ()),
            }
            for i, b in enumerate((2, 1, 0)):
                for half in range(2):
                    w = (("bm_ps", 4),) if i == 0 else (("mixed", 2 * i),)
                    L1[f"g{b}{half}"] = (gate[:, :, half * 512:(half + 1) * 512], ACT.Exp, -1.0, w)
                    no = 2 * i + half
                    w = (("cv_y", 1),) if no == 0 else (("mixed", no),)
                    L1[f"u{b}{half}"] = (up_e, ACT.Copy, 1.0, w)
            ends = {last_unit(n): n for n in L1}
            for u in range(JOBS["wo0"]["u0"]):
                hi(u + LEAD)
                if u in ends:
                    evac(ends[u], *L1[ends[u]])
                if u == 8:
                    rsqrt(rs20, nt20, "qk_v", 1, "qk_r")
                if u == 9:
                    act.wait_ge(sem("qk_tr"), 1)
                    act.activation(kTd, ps[:, W0, 0:S], ACT.Copy, scale=sml[:, G_K:G_K + 1])
                    act.activation(qTd, ps[:, W1:W1 + 2, :].rearrange("p a (b c) -> p (a b) c", b=2), ACT.Copy,
                                   scale=g8).then_inc(sem("qk_T"), 1)
                if u == 10:
                    for t in range(TT):
                        act.wait_ge(sem("idx"), t + 1)
                        b, w = (W2, P) if t == 0 else (W0, S)
                        act.activation((ir0 if t == 0 else ir1).rearrange("p (a b) c -> p a (b c)", a=2),
                                       ps[:, b:b + 2, 0:2 * w], ACT.Relu).then_inc(sem("idx_r"), 1)
                if 24 <= u < 40:
                    att_step(0, u - 24)
                if u == 40:
                    act.wait_ge(sem("hg_e1"), 1)
                    link(act.activation(hE, hE, ACT.Exp))
                    act.activation(hE, hE, ACT.Ln, bias=bias1).then_inc(sem("hg_ln"), 1)
                if u == 41:
                    act.wait_ge(sem("hg_c"), 1)
                    link(act.activation(hz, hz, ACT.Exp, scale=-1.0))
                    act.activation(hF, hW, ACT.Exp, scale=-1.0)
                    link(act.activation(hdT, c3(hE, a=32)[:, :, HB - 1], ACT.Exp, scale=-1.0))
                    link(act.activation(hW, hW, ACT.Exp))
                    act.activation(hE, hE, ACT.Exp, scale=-1.0)
                    act.activation(hX, hX, ACT.Exp, scale=-1.0).then_inc(sem("hg_e2"), 1)
                if 42 <= u < 54:
                    hd, stage = divmod(u - 42, 3)
                    if stage == 0:
                        act.wait_ge(sem("hg_kt"), hd + 1)
                        act.activation(khT[:, :, hd * P:(hd + 1) * P],
                                       ps[:, W1, 0:S].rearrange("p (a b) -> p a b", a=TT),
                                       ACT.Copy).then_inc(sem("hg_ktc"), 1)
                    if stage == 2:
                        act.wait_ge(sem("hg_o"), hd + 1)
                        act.activation(o_all[:, :, hd * P:(hd + 1) * P],
                                       ps[:, W3, 0:S].rearrange("p (a b) -> p a b", a=TT),
                                       ACT.Copy).then_inc(sem("hg_oc"), 1)
                if u == 54:
                    act.activation(hE, hgt.rearrange("p a b -> p (a b)"), ACT.Exp, scale=-1.0).then_inc(sem("hg_sg"), 1)
                    rsqrt(rs20[:, 0:8], nt20[:, 0:8], "hg_v", 1, "hg_r")
                if u == 54:
                    y_hi(0, 0)
                if u == 57:
                    y_hi(1, 1)
                if u == 44:
                    act.wait_ge(sem("cv_y"), 1)
                    act.activation(Y[0][:, 0, :, :], cv_y, ACT.Copy).then_inc(sem("cv_hi"), 1)
            for b in range(4):
                act.wait_ge(sem("mx_tr"), b + 1)
                act.activation(hT[0][:, 2 * b:2 * b + 2, :], ps[:, W0 + b, :], ACT.Copy).then_inc(sem("mx_hi"), 1)
            for u in range(JOBS["wo0"]["u0"], JOBS["mlp0"]["u0"]):
                hi(u + LEAD)

            def mlp(i):
                base = JOBS[f"mlp{i}"]["u0"]

                def up(g, u):
                    r = relu[:, g % 2, :]
                    b = 2 * ((pair_of[f"mlp{i}"] + g) % 2)
                    act.wait_ge(sem("used"), u + 4)
                    if g >= 2:
                        act.wait_ge(sem("m_sq"), NG * i + g - 1)
                    act.activation(r, ps[:, b:b + 2, :].rearrange("p a b -> p (a b)"), ACT.Relu).then_inc(sem("evac"), 1)
                    act.wait_ge(sem("evac"), evac_no[f"mlp{i}"] + g + 1)
                    if g >= 2:
                        act.wait_ge(sem("used"), base + 8 * (g - 1) + 4)
                    act.activation(Y[0][:, g % 2, :, :], c3(r, a=4), ACT.Square).then_inc(sem("m_hi"), 1)

                g = 0
                for k in range(NG * 8):
                    hi(base + k + LEAD)
                    if k == 3:
                        up(0, base)
                    elif k % 8 == 7 and k < NG * 8 - 1:
                        g += 1
                        up(g, base + 8 * g - 4)

            norm(1)
            mlp(0)
            norm(2)
            L2 = {"fa": (fa, ACT.Copy, 1.0), "fq": (fq, ACT.Copy, 0.125), "fk": (fk, ACT.Copy, 1.0),
                  "fv": (fv, ACT.Copy, 1.0), "bq": (bq, ACT.Copy, 0.125), "bk": (bk, ACT.Copy, 1.0),
                  "bv": (bv, ACT.Copy, 1.0)}
            ends = {last_unit(n): n for n in L2}
            base = JOBS["fa"]["u0"]
            for u in range(25):
                hi(base + u + LEAD)
                if base + u in ends:
                    evac(ends[base + u], *L2[ends[base + u]])
                if u == 1:
                    act.wait_ge(sem("fx_e"), 1)
                    link(act.activation(nt20[:, 0:16], st20[:, 0:16], ACT.Exp))
                    act.activation(nt20[:, 0:16], nt20[:, 0:16], ACT.Ln, bias=bias1).then_inc(sem("fx_ln"), 1)
                if 13 <= u < 25:
                    for n in range((u - 13) * 4 // 3, (u - 12) * 4 // 3):
                        att_step(1, n)
            y_hi(2, 0)
            for n in range(16):
                if n % 4 == 0:
                    hi(base + 25 + n // 4 + LEAD)
                att_step(2, n)
            y_hi(3, 1)
            for u in range(29, 33):
                hi(base + u + LEAD)
            norm(3)
            mlp(1)
            norm(4)
            base = JOBS["cq"]["u0"]
            L3 = {"cq": (cqt, ACT.Copy, 1.0), "ckv": (ckt, ACT.Copy, 1.0), "sq": (sq, ACT.Copy, 0.125),
                  "sk": (sk, ACT.Copy, 1.0), "uq0": (qtk[:, :, 0:512], ACT.Copy, 1.0),
                  "uq1": (qtk[:, :, 512:768], ACT.Copy, 1.0), "kn": (knt, ACT.Copy, 1.0),
                  "vn": (vnt, ACT.Copy, 1.0), "sv": (sv, ACT.Copy, 1.0)}
            ends = {last_unit(n): n for n in L3}
            n3 = JOBS["wob"]["u0"] - base
            for u in range(n3):
                hi(base + u + LEAD)
                if base + u in ends:
                    evac(ends[base + u], *L3[ends[base + u]])
                if u == 8:
                    act.wait_ge(sem("ro_a"), 1)
                    act.activation(rot, rot, ACT.Sin).then_inc(sem("ro_s"), 1)
                    act.preload_act_table_set("natural_log_exp_and_others")
                    rsqrt(rs20[:, 0:4], nt20[:, 0:4], "la_v", 1, "la_r")
                if u == 9:
                    act.wait_ge(sem("la_tr"), 1)
                    for kt in range(3):
                        act.activation(Y[0][:, 0, kt, :], ps[:, W0 + kt // 2, (kt % 2) * S:(kt % 2 + 1) * S], ACT.Copy,
                                       scale=sml[:, G_CQ + kt:G_CQ + kt + 1])
                    for kt in range(2):
                        m = act.activation(Y[0][:, 1, kt, :], ps[:, W2, kt * S:(kt + 1) * S], ACT.Copy,
                                           scale=sml[:, G_CKV + kt:G_CKV + kt + 1])
                    m.then_inc(sem("la_hi"), 1)

            def sb_first(h):
                t = sbt[:, h % 2, :]
                act.wait_ge(sem("sb_m"), h + 1)
                link(act.activation(t, t, ACT.Exp))
                act.activation(t, t, ACT.Ln, bias=bias1).then_inc(sem("sb_l"), 1)

            def sb_second(h):
                act.wait_ge(sem("sb_r"), h + 1)
                act.activation(sbt[:, h % 2, :], ps[:, W0 + h % 2, 0:384], ACT.Exp).then_inc(sem("sb_a"), 1)
                if h % 2:
                    act.wait_ge(sem("sb_v"), h + 1)
                    act.activation(Y[0][:, 0, h // 2, :], ps[:, W2 + (h // 2) % 2, 0:S],
                                   ACT.Copy).then_inc(sem("sb_hi"), 1)

            sb_first(0)
            for h in range(8):
                if h < 7:
                    sb_first(h + 1)
                sb_second(h)
            for c, (dst, scale) in enumerate(((qTm, 96.0 ** -0.5), (qTm, 96.0 ** -0.5), (kTm, 1.0), (kTm, 1.0))):
                act.wait_ge(sem("ml_tr"), c + 1)
                h = 4 * (c % 2)
                act.activation(dst[0:96, h:h + 4, :], ps[0:96, W2:W2 + 2, :].rearrange("p a (b c) -> p (a b) c", b=2),
                               ACT.Copy, scale=scale).then_inc(sem("ml_T"), 1)
            for n in range(16):
                if n % 4 == 0:
                    hi(base + n3 + n // 4 + LEAD)
                att_step(3, n)
            y_hi(4, 1)
            for u in range(4, 8):
                hi(base + n3 + u + LEAD)
            norm(5)
            mlp(2)
            norm(6)

        @block.gpsimd
        def _(pool):
            pool.memset(hA, 0.0)
            pool.memset(hMask, 1.0).then_inc(sem("pl_link"), 1)
            pool.wait_ge(sem("pl_link"), 1)
            pool.memset(c3(hMask, a=NHB)[:, :, 0], 0.0).then_inc(sem("pl_c"), 1)
            pool.wait_ge(sem("c_in"), 32)
            pool.wait_ge(sem("evac"), evac_no["hi"] + 1)
            for hd in range(4):
                for t in range(TT):
                    if hd >= 1:
                        pool.wait_ge(sem("hg_u"), TT * hd)
                    m = pool.tensor_tensor(i4[:, t, :].rearrange("p (a b) -> p a b", a=4),
                                           hin[:, t, hd * P:(hd + 1) * P].unsqueeze(1).to_broadcast([P, 4, P]),
                                           cst[:, C_BLK:C_BLK + 4].unsqueeze(2).to_broadcast([P, 4, P]), ALU.mult)
                m.then_inc(sem("hg_i4"), 1)
            for i, b in enumerate((2, 1, 0)):
                pool.wait_ge(sem("evac"), evac_no[f"g{b}1"] + 1)
                g = gate.rearrange("p a b -> p (a b)")
                pool.tensor_scalar(g, g, 1.0, None, ALU.add).then_inc(sem("g_1"), 1)

        @block.vector
        def _(dve):
            link_no = [0]

            def link(i):
                link_no[0] += 1
                i.then_inc(sem("dve_link"), 1)
                dve.wait_ge(sem("dve_link"), link_no[0])

            def lo(u):
                if u >= UNITS:
                    return
                dve.wait_ge(sem("hi_done"), u + 1)
                dve.tensor_tensor(wlo[:, u % RING, :], raw[:, u % RAW, :], whi[:, u % RING, :].bitcast(F32),
                                  ALU.subtract).then_inc(sem("lo_done"), 1)

            def refine(r, v, tmp):
                link(dve.tensor_tensor(tmp, r, r, ALU.mult))
                link(dve.tensor_tensor(tmp, tmp, v, ALU.mult))
                link(dve.tensor_scalar(tmp, tmp, -0.5, 1.5, ALU.mult, ALU.add))
                link(dve.tensor_tensor(r, r, tmp, ALU.mult))

            tmp2 = stat[:, 6:8]
            x_n = arena[:, 0:2048].rearrange("p (a b) -> p a b", a=TT)

            def norm(i):
                dve.wait_ge(sem("n_ss"), TT * (i + 1))
                dve.tensor_scalar(nt, ss, 1.0 / D, EPS, ALU.mult, ALU.add).then_inc(sem("n_v"), 1)
                dve.wait_ge(sem("n_r"), i + 1)
                refine(rs, nt, tmp2)
                for t in range(TT):
                    if i < len(NORMS):
                        dve.tensor_scalar(x_n[:, t, :], x[:, t, :], rs[:, t:t + 1], None,
                                          ALU.mult).then_inc(sem("n_x"), 1)
                    else:
                        if t == 0:
                            dve.wait_ge(sem("g_in"), 16)
                        dve.scalar_tensor_tensor(x[:, t, :], x[:, t, :], rs[:, t:t + 1], gbc, ALU.mult,
                                                 ALU.mult).then_inc(sem("y_out"), 1)
                if i == len(NORMS):
                    return
                for b in range(4):
                    dve.wait_ge(sem("n_hi"), 4 * i + b + 1)
                    for k in (2 * b, 2 * b + 1):
                        m = dve.scalar_tensor_tensor(hT[1][:, k, :], ps[:, W0 + b, (k % 2) * S:(k % 2 + 1) * S],
                                                     sml[:, GAIN[i] + k:GAIN[i] + k + 1],
                                                     hT[0][:, k, :].bitcast(F32), ALU.mult, ALU.subtract)
                    m.then_inc(sem("n_lo"), 1)

            def att_step(a, n, bias):
                t, h = divmod(n, 8)
                N = 16 * a + n
                w = P * (t + 1)
                dve.wait_ge(sem("att_qk"), N + 1)
                if n >= 2:
                    dve.wait_ge(sem("att_exp"), N - 1)
                link(dve.tensor_tensor_reduce(Lb[:, n % 2, 0:w], ps[:, W0 + n % 2, 0:w], bias(h, t), 1.0, -3e38,
                                              ALU.add, ALU.max, mx[:, n:n + 1]))
                dve.tensor_scalar(nmx[:, n:n + 1], mx[:, n:n + 1], -1.0, None, ALU.mult).then_inc(sem("att_nmx"), 1)

            def att_close(a, t, y):
                N = 16 * a + 8 * t
                dve.wait_ge(sem("att_exp"), N + 8)
                link(dve.reciprocal(rsum[:, 8 * t:8 * t + 8], sums[:, 8 * t:8 * t + 8]))
                dve.wait_ge(sem("att_pv"), N + 8)
                i = dve.tensor_tensor(y[:, t, :].rearrange("p (a b) -> p a b", a=8),
                                      ps[:, W3, :].rearrange("p (a b) -> p a b", a=8),
                                      rsum[:, 8 * t:8 * t + 8].unsqueeze(2).to_broadcast([P, 8, 64]), ALU.mult)
                i.then_inc(sem("att_on"), 1)

            def y_lo(no, slot):
                dve.wait_ge(sem("y_hi"), no + 1)
                for b in range(2):
                    m = dve.tensor_tensor(Y[1][:, slot, 2 * b:2 * b + 2, :], ps[:, W0 + b, :].rearrange("p (a b) -> p a b", a=2),
                                          Y[0][:, slot, 2 * b:2 * b + 2, :].bitcast(F32), ALU.subtract)
                m.then_inc(sem("y_lo"), 1)

            for u in range(LEAD):
                lo(u)
            norm(0)
            dve.memset(bias1, 1.0)
            dve.tensor_scalar(g8, sml[:, G_Q:G_Q + 1], 0.125, None, ALU.mult)

            def topk(t, r):
                s = isc[:, 0:P] if t == 0 else isc[:, P:3 * P]
                link(dve.max(top8, s))
                link(dve.match_replace(s, top8, s, TAKEN))

            def conv_tap(ct):
                c = ccT[:, ct, :]
                acc = chT[:, ct, :]
                w = sml[:, G_CONV + 3 * ct:G_CONV + 3 * ct + 3]
                link(dve.tensor_tensor(c, c, acc, ALU.mult))
                link(dve.tensor_scalar(acc, c, w[:, 2:3], None, ALU.mult))
                link(dve.scalar_tensor_tensor(acc[:, 1:S], c[:, 0:S - 1], w[:, 1:2], acc[:, 1:S], ALU.mult, ALU.add))
                link(dve.scalar_tensor_tensor(acc[:, 2:S], c[:, 0:S - 2], w[:, 0:1], acc[:, 2:S], ALU.mult, ALU.add))
                m = dve.tensor_tensor(cv_y[:, ct, :], cbT[:, ct, :], acc, ALU.mult)
                if ct == 3:
                    m.then_inc(sem("cv_y"), 1)
                else:
                    link(m)

            def flat(v):
                return v.rearrange("p a b -> p (a b)")

            def mix(no):
                half = no % 2
                m = mixed[:, :, half * 512:(half + 1) * 512]
                g = gate[:, :, half * 512:(half + 1) * 512]
                name = f"u{2 - no // 2}{half}"
                if half == 0:
                    dve.wait_ge(sem("g_1"), no // 2 + 1)
                    link(dve.reciprocal(flat(gate), flat(gate)))
                dve.wait_ge(sem("evac"), evac_no[name] + 1)
                if no < 2:
                    dve.tensor_tensor(m, up_e, g, ALU.mult).then_inc(sem("mixed"), 1)
                else:
                    link(dve.tensor_tensor(up_t, up_e, g, ALU.mult))
                    dve.tensor_tensor(m, m, up_t, ALU.add).then_inc(sem("mixed"), 1)

            for u in range(JOBS["wo0"]["u0"]):
                lo(u + LEAD)
                if u == 7:
                    dve.wait_ge(sem("evac"), evac_no["akv"] + 1)
                    link(dve.tensor_tensor(hE, flat(qraw), flat(qraw), ALU.mult))
                    link(dve.tensor_reduce(st20[:, 0:16], c3(hE, a=16), AX.X, ALU.add))
                    e4 = hE[:, 0:256].rearrange("p (a b c) -> p a b c", a=TT, b=2)
                    k4 = kvw[:, :, 0:P].rearrange("p a (b c) -> p a b c", b=2)
                    link(dve.tensor_tensor(e4, k4, k4, ALU.mult))
                    link(dve.tensor_reduce(st20[:, 16:20], c3(hE[:, 0:256], a=4), AX.X, ALU.add))
                    dve.tensor_scalar(nt20, st20, 1.0 / 64, EPS, ALU.mult, ALU.add).then_inc(sem("qk_v"), 1)
                if u == 8:
                    dve.wait_ge(sem("qk_r"), 1)
                    refine(rs20, nt20, st20)
                    q16 = flat(qraw).rearrange("p (a b) -> p a b", a=16)
                    dve.tensor_tensor(q16, q16, rs20[:, 0:16].unsqueeze(2).to_broadcast([P, 16, 64]), ALU.mult)
                    k4 = kvw[:, :, 0:P].rearrange("p a (b c) -> p a b c", b=2)
                    r4 = rs20[:, 16:20].rearrange("p (a b) -> p a b", a=TT).unsqueeze(3).to_broadcast([P, TT, 2, 64])
                    dve.tensor_tensor(k4, k4, r4, ALU.mult).then_inc(sem("qk_n"), 1)
                    link(dve.tensor_scalar(wi, kvw[:, :, 256:260], 1.0 / 16, None, ALU.mult))
                if u == 11:
                    for t in range(TT):
                        dve.wait_ge(sem("idx_r"), t + 1)
                        s = isc[:, 0:P] if t == 0 else isc[:, P:3 * P]
                        r = ir0 if t == 0 else ir1
                        mk = cs(C_CM) if t == 0 else cst[:, C_Z:C_Z + S]
                        link(dve.scalar_tensor_tensor(s, r[:, 0, :], wi[:, t, 0:1], mk, ALU.mult, ALU.add))
                        for h in range(1, 4):
                            link(dve.scalar_tensor_tensor(s, r[:, 2 * (h % 2) + h // 2, :], wi[:, t, h:h + 1], s,
                                                          ALU.mult, ALU.add))
                if 12 <= u < 20:
                    topk(0, u - 12)
                    topk(1, u - 12)
                if u == 20:
                    link(dve.tensor_scalar(imask, isc, -2e38, NEG, ALU.is_gt, ALU.mult))
                    dve.tensor_tensor(imask[:, 0:P], imask[:, 0:P], cs(C_CM), ALU.add)
                    link(dve.tensor_tensor(imask[:, S:S + P], imask[:, S:S + P], cs(C_CM), ALU.add))
                if u == 22:
                    for g in range(4):
                        dve.wait_ge(sem("bm_ps"), g + 1)
                        b2 = ps[:, W0 + g, :].rearrange("p (a b) -> p a b", a=2)
                        dve.tensor_tensor(bm[:, 2 * g:2 * g + 2, 0:P], b2[:, :, P:S],
                                          imask[:, 0:P].unsqueeze(1).to_broadcast([P, 2, P]), ALU.add)
                        m = dve.tensor_tensor(bm[:, 2 * g:2 * g + 2, P:3 * P], b2,
                                              imask[:, P:3 * P].unsqueeze(1).to_broadcast([P, 2, S]), ALU.add)
                    m.then_inc(sem("bm_ok"), 1)
                    dve.wait_ge(sem("bm_ok"), 1)
                if 24 <= u < 40:
                    att_step(0, u - 24, lambda h, t: bm[:, h, 0:P] if t == 0 else bm[:, h, P:3 * P])
                    if u == 33:
                        att_close(0, 0, y_tok)
                if u in (34, 36, 38, 40):
                    if u == 34:
                        dve.wait_ge(sem("evac"), evac_no["cb"] + 1)
                    conv_tap((u - 34) // 2)
                if u == 39:
                    dve.wait_ge(sem("evac"), evac_no["hq"] + 1)
                    dve.tensor_scalar(hE, flat(hz), -1.0, 30.0, ALU.mult, ALU.min).then_inc(sem("hg_e1"), 1)
                if u == 40:
                    att_close(0, 1, y_tok)
                    dve.wait_ge(sem("hg_ln"), 1)
                    link(dve.scalar_tensor_tensor(hW, flat(hz), -1.0, hE, ALU.mult, ALU.max))
                    dve.wait_ge(sem("pl_c"), 1)
                    dve.tensor_tensor(flat(hz), flat(hz), hW, ALU.add)
                    for hd in range(4):
                        m = dve.tensor_tensor_scan(hE[:, hd * S:(hd + 1) * S], hMask, hW[:, hd * S:(hd + 1) * S], 0.0,
                                                   ALU.mult, ALU.add)
                    link(m)
                    c32 = c3(hE, a=32)
                    mid = c32[:, :, HB // 2 - 1:HB // 2].to_broadcast([P, 32, HB])
                    end = c32[:, :, HB - 1:HB].to_broadcast([P, 32, HB])
                    link(dve.tensor_tensor(c3(hW, a=32), c32, mid, ALU.subtract))
                    link(dve.tensor_scalar(hW, hW, 85.0, -85.0, ALU.min, ALU.max))
                    dve.tensor_tensor(c3(hX, a=32), end, c32, ALU.subtract).then_inc(sem("hg_c"), 1)
                if u == 41:
                    dve.wait_ge(sem("hg_e2"), 1)
                    dve.tensor_tensor(hF, hF, flat(hqf), ALU.mult)
                    dve.tensor_tensor(hE, hE, flat(hqf), ALU.mult)
                    dve.tensor_tensor(hW, hW, flat(hz), ALU.mult)
                    dve.tensor_tensor(hX, hX, flat(hz), ALU.mult).then_inc(sem("hg_f"), 1)
                if 42 <= u < 54:
                    hd, stage = divmod(u - 42, 3)
                    if stage == 0:
                        dve.wait_ge(sem("hg_a"), hd + 1)
                        if hd >= 1:
                            dve.wait_ge(sem("hg_o"), hd)
                        for t in range(TT):
                            m = dve.copy_predicated(hA[:, t, :], cs(C_BD).bitcast(I32), ps[:, W0, t * P:(t + 1) * P])
                        m.then_inc(sem("hg_am"), 1)
                    if stage == 1:
                        for n in range(7):
                            b = W2 if n < 4 else W1
                            if n % 4 == 0:
                                dve.wait_ge(sem("hg_u"), TT * hd + n // 4 + 1)
                            src = ps[:, b, (n % 4) * P:(n % 4 + 1) * P]
                            if n == 0:
                                m = dve.tensor_copy(hS[:, 1, :], src)
                            else:
                                m = dve.scalar_tensor_tensor(hS[:, n + 1, :], hS[:, n, :], hdT[:, 8 * hd + n:8 * hd + n + 1],
                                                             src, ALU.mult, ALU.add)
                            m.then_inc(sem("hg_s"), 1)
                            dve.wait_ge(sem("hg_s"), 7 * hd + n + 1)
                if u == 45:
                    dve.wait_ge(sem("cv_hi"), 1)
                    dve.tensor_tensor(Y[1][:, 0, :, :], cv_y, Y[0][:, 0, :, :].bitcast(F32),
                                      ALU.subtract).then_inc(sem("y_lo"), 1)
                if u == 53:
                    dve.wait_ge(sem("hg_oc"), 4)
                    link(dve.tensor_tensor(hX, flat(o_all), flat(o_all), ALU.mult))
                    link(dve.tensor_reduce(st20[:, 0:8], c3(hX, a=8), AX.X, ALU.add))
                    dve.tensor_scalar(nt20[:, 0:8], st20[:, 0:8], 1.0 / P, EPS, ALU.mult, ALU.add).then_inc(sem("hg_v"), 1)
                if u == 48:
                    mix(0)
                if u == 50:
                    mix(1)
                if u == 54:
                    y_lo(0, 0)
                    dve.wait_ge(sem("hg_sg"), 1)
                    link(dve.tensor_scalar(hE, hE, 1.0, None, ALU.add))
                    link(dve.reciprocal(hE, hE))
                    link(dve.tensor_tensor(hE, hE, flat(hgt), ALU.mult))
                    dve.wait_ge(sem("hg_r"), 1)
                    refine(rs20[:, 0:8], nt20[:, 0:8], st20[:, 0:8])
                if u == 55:
                    e8 = c3(hE, a=8)
                    o8 = flat(o_all).rearrange("p (a b) -> p a b", a=8)
                    link(dve.tensor_tensor(e8, e8, sml[:, G_H:G_H + P].unsqueeze(1).to_broadcast([P, 8, P]), ALU.mult))
                    link(dve.tensor_tensor(e8, e8, rs20[:, 0:8].unsqueeze(2).to_broadcast([P, 8, P]), ALU.mult))
                if u == 56:
                    dve.tensor_tensor(hF, flat(o_all), hE, ALU.mult).then_inc(sem("hg_y"), 1)
                if u == 57:
                    y_lo(1, 1)
                if u == 60:
                    mix(2)
                if u == 62:
                    mix(3)
                if u == 72:
                    mix(4)
                if u == 73:
                    mix(5)
            for b in range(4):
                dve.wait_ge(sem("mx_hi"), b + 1)
                dve.tensor_tensor(hT[1][:, 2 * b:2 * b + 2, :], ps[:, W0 + b, :].rearrange("p (a b) -> p a b", a=2),
                                  hT[0][:, 2 * b:2 * b + 2, :].bitcast(F32), ALU.subtract).then_inc(sem("mx_lo"), 1)
            for u in range(JOBS["wo0"]["u0"], JOBS["mlp0"]["u0"]):
                lo(u + LEAD)

            def residual(b0, b1, last):
                dve.wait_ge(sem("used"), last + 1)
                for t in range(TT):
                    for half, b in ((0, b0), (1, b1)):
                        v = x[:, t, half * 512:(half + 1) * 512]
                        m = dve.tensor_tensor(v, v, ps[:, b + t, :], ALU.add)
                    m.then_inc(sem("x_ok"), 1)

            pair_of, c = {}, 0
            for n in JOBS:
                pair_of[n] = c % 2
                c += {"M": NG, "O": 2}.get(JOBS[n]["kind"], 1)
            residual(2 * pair_of["wo0"], 2 * pair_of["wo1"], last_unit("wo1"))

            def mlp(i):
                base = JOBS[f"mlp{i}"]["u0"]

                def up(g):
                    r = relu[:, g % 2, :]
                    dve.wait_ge(sem("evac"), evac_no[f"mlp{i}"] + g + 1)
                    if g >= 1:
                        dve.wait_ge(sem("m_lo"), NG * i + g)
                    dve.tensor_tensor(sqr, r, r, ALU.mult).then_inc(sem("m_sq"), 1)
                    dve.wait_ge(sem("m_sq"), NG * i + g + 1)
                    dve.wait_ge(sem("m_hi"), NG * i + g + 1)
                    dve.tensor_tensor(Y[1][:, g % 2, :, :], c3(sqr, a=4), Y[0][:, g % 2, :, :].bitcast(F32),
                                      ALU.subtract).then_inc(sem("m_lo"), 1)

                g = 0
                for k in range(NG * 8):
                    lo(base + k + LEAD)
                    if k == 3:
                        up(0)
                    elif k % 8 == 7 and k < NG * 8 - 1:
                        g += 1
                        up(g)
                residual(W0, W2, base + NG * 8 - 1)

            norm(1)
            mlp(0)
            norm(2)
            base = JOBS["fa"]["u0"]
            causal = (cs(C_CM), cst[:, C_Z:C_Z + S])
            chunked = (cs(C_CK), cst[:, C_Z2:C_Z2 + S])
            for u in range(25):
                lo(base + u + LEAD)
                if u == 1:
                    dve.wait_ge(sem("evac"), evac_no["fa"] + 1)
                    link(dve.tensor_tensor(fa, fa, sml[:, G_BF:G_BF + 8].unsqueeze(1).to_broadcast([P, TT, 8]), ALU.add))
                    f = flat(fa)
                    dve.tensor_scalar(st20[:, 0:16], f, -1.0, 30.0, ALU.mult, ALU.min).then_inc(sem("fx_e"), 1)
                    dve.wait_ge(sem("fx_ln"), 1)
                    dve.scalar_tensor_tensor(f, f, -1.0, nt20[:, 0:16], ALU.mult, ALU.max).then_inc(sem("fx_n"), 1)
                    dve.wait_ge(sem("fx_cn"), 1)
                    link(dve.tensor_copy(cnq, ps[:, W0, 0:16]))
                if 3 <= u < 11:
                    h = u - 3
                    b = W1 + h % 2
                    dve.wait_ge(sem("fx_bc"), h + 1)
                    dve.scalar_tensor_tensor(bm[:, h, 0:P], ps[:, b, 0:P], cnq[:, h:h + 1], causal[0],
                                             ALU.subtract, ALU.add)
                    dve.scalar_tensor_tensor(bm[:, h, P:3 * P], ps[:, b, 0:S], cnq[:, 8 + h:9 + h], causal[1],
                                             ALU.subtract, ALU.add).then_inc(sem("fx_bm"), 1)
                if u == 11:
                    dve.wait_ge(sem("fx_bm"), 8)
                    for g in range(4):
                        dve.wait_ge(sem("bm_ps"), 4 + g + 1)
                        b2 = ps[:, W0 + g, :].rearrange("p (a b) -> p a b", a=2)
                        dve.tensor_tensor(bm2[:, 2 * g:2 * g + 2, 0:P], b2[:, :, P:S],
                                          chunked[0].unsqueeze(1).to_broadcast([P, 2, P]), ALU.add)
                        m = dve.tensor_tensor(bm2[:, 2 * g:2 * g + 2, P:3 * P], b2,
                                              chunked[1].unsqueeze(1).to_broadcast([P, 2, S]), ALU.add)
                    m.then_inc(sem("bm_ok"), 1)
                    dve.wait_ge(sem("bm_ok"), 2)
                if 13 <= u < 25:
                    for n in range((u - 13) * 4 // 3, (u - 12) * 4 // 3):
                        att_step(1, n, lambda h, t: bm[:, h, 0:P] if t == 0 else bm[:, h, P:3 * P])
                        if n == 9:
                            att_close(1, 0, y2)
            att_close(1, 1, y2)
            y_lo(2, 0)
            for n in range(16):
                if n % 4 == 0:
                    lo(base + 25 + n // 4 + LEAD)
                att_step(2, n, lambda h, t: bm2[:, h, 0:P] if t == 0 else bm2[:, h, P:3 * P])
                if n == 9:
                    att_close(2, 0, y2)
            att_close(2, 1, y2)
            y_lo(3, 1)
            for u in range(29, 33):
                lo(base + u + LEAD)
            p0 = 2 * pair_of["woa"]
            residual(p0, 2 - p0, last_unit("woa"))
            norm(3)
            mlp(1)
            norm(4)

            base = JOBS["cq"]["u0"]
            n3 = JOBS["wob"]["u0"] - base
            r64 = rot.rearrange("p t n -> p (t n)")
            ang = rtmp[:, 0:64]
            turns = rtmp[:, 64:128]
            for u in range(n3):
                lo(base + u + LEAD)
                if u == 5:
                    dve.wait_ge(sem("p_in"), 16)
                    link(dve.tensor_copy(ss, posi[:]))
                    for t in range(TT):
                        for c in range(2):
                            m = dve.tensor_scalar(ang[:, (2 * t + c) * 16:(2 * t + c + 1) * 16], cst[:, C_FREQ:C_FREQ + 16],
                                                  ss[:, t:t + 1], None, ALU.mult)
                    link(m)
                    link(dve.tensor_scalar(turns, ang, 1.0 / (2 * np.pi), None, ALU.mult))
                    cosines = turns.rearrange("p (t c n) -> p t c n", t=TT, c=2)[:, :, 1, :]
                    link(dve.tensor_scalar(cosines, cosines, 0.25, None, ALU.add))
                    link(dve.tensor_scalar(turns, turns, MAGIC, None, ALU.add))
                    link(dve.tensor_scalar(turns, turns, -MAGIC, None, ALU.add))
                    for part in TURN:
                        link(dve.scalar_tensor_tensor(ang, turns, -part, ang, ALU.mult, ALU.add))
                    cosines = ang.rearrange("p (t c n) -> p t c n", t=TT, c=2)[:, :, 1, :]
                    link(dve.tensor_scalar(cosines, cosines, np.pi / 2, None, ALU.add))
                    dve.tensor_scalar(r64, ang, 3.1415925, -3.1415925, ALU.min, ALU.max).then_inc(sem("ro_a"), 1)
                if u == 7:
                    dve.wait_ge(sem("evac"), evac_no["ckv"] + 1)
                    big = kfl.rearrange("p a b -> p (a b)")
                    s0, s1 = big[:, 0:768].rearrange("p (a b) -> p a b", a=TT), big[:, 768:1280].rearrange("p (a b) -> p a b", a=TT)
                    dve.tensor_tensor(s0, cqt, cqt, ALU.mult)
                    link(dve.tensor_tensor(s1, ckt[:, :, 0:256], ckt[:, :, 0:256], ALU.mult))
                    dve.tensor_reduce(st20[:, 0:2], s0, AX.X, ALU.add)
                    link(dve.tensor_reduce(st20[:, 2:4], s1, AX.X, ALU.add))
                    dve.tensor_scalar(nt20[:, 0:2], st20[:, 0:2], 1.0 / 384, EPS, ALU.mult, ALU.add)
                    dve.tensor_scalar(nt20[:, 2:4], st20[:, 2:4], 1.0 / 256, EPS, ALU.mult, ALU.add).then_inc(sem("la_v"), 1)
                    dve.wait_ge(sem("la_v"), 1)
                if u == 8:
                    dve.wait_ge(sem("la_r"), 1)
                    refine(rs20[:, 0:4], nt20[:, 0:4], st20[:, 0:4])
                    for t in range(TT):
                        dve.tensor_scalar(cqt[:, t, :], cqt[:, t, :], rs20[:, t:t + 1], None, ALU.mult)
                        m = dve.tensor_scalar(ckt[:, t, 0:256], ckt[:, t, 0:256], rs20[:, 2 + t:3 + t], None, ALU.mult)
                    m.then_inc(sem("la_n"), 1)
                if u == 9:
                    dve.wait_ge(sem("la_hi"), 1)
                    for kt in range(3):
                        dve.scalar_tensor_tensor(Y[1][:, 0, kt, :], ps[:, W0 + kt // 2, (kt % 2) * S:(kt % 2 + 1) * S],
                                                 sml[:, G_CQ + kt:G_CQ + kt + 1], Y[0][:, 0, kt, :].bitcast(F32),
                                                 ALU.mult, ALU.subtract)
                    for kt in range(2):
                        m = dve.scalar_tensor_tensor(Y[1][:, 1, kt, :], ps[:, W2, kt * S:(kt + 1) * S],
                                                     sml[:, G_CKV + kt:G_CKV + kt + 1], Y[0][:, 1, kt, :].bitcast(F32),
                                                     ALU.mult, ALU.subtract)
                    m.then_inc(sem("la_lo"), 1)
                if u == 19:
                    dve.wait_ge(sem("ro_s"), 1)
                    dve.wait_ge(sem("evac"), evac_no["uq1"] + 1)

                    def rotate(x1, x2, t, heads):
                        n = 16 * heads
                        v = [rtmp[:, 128 * i:128 * i + n].rearrange("p (h n) -> p h n", h=heads) for i in range(4)]
                        sn = rot[:, t, 0:16].unsqueeze(1).to_broadcast([P, heads, 16])
                        cn = rot[:, t, 16:32].unsqueeze(1).to_broadcast([P, heads, 16])
                        dve.tensor_tensor(v[0], x1, cn, ALU.mult)
                        dve.tensor_tensor(v[1], x2, sn, ALU.mult)
                        dve.tensor_tensor(v[2], x2, cn, ALU.mult)
                        link(dve.tensor_tensor(v[3], x1, sn, ALU.mult))
                        dve.tensor_tensor(x1, v[0], v[1], ALU.subtract)
                        return dve.tensor_tensor(x2, v[2], v[3], ALU.add)

                    for t in range(TT):
                        q8 = qtk[:, t, :].rearrange("p (h n) -> p h n", h=8)
                        m = rotate(q8[:, :, 64:80], q8[:, :, 80:96], t, 8)
                        m.then_inc(sem("ro_q"), 1)
                        dve.wait_ge(sem("ro_q"), t + 1)
                if u == 20:
                    dve.wait_ge(sem("evac"), evac_no["kn"] + 1)
                    for t in range(TT):
                        k1 = ckt[:, t, 256:272].unsqueeze(1)
                        k2 = ckt[:, t, 272:288].unsqueeze(1)
                        link(rotate(k1, k2, t, 1))
                        k8 = kfl[:, t, :].rearrange("p (h n) -> p h n", h=8)
                        dve.tensor_copy(k8[:, :, 64:96], ckt[:, t, 256:288].unsqueeze(1).to_broadcast([P, 8, 32]))
                        m = dve.tensor_copy(k8[:, :, 0:64], knt[:, t, :].rearrange("p (h n) -> p h n", h=8))
                    m.then_inc(sem("ro_k"), 1)

            def sb_first(h):
                dve.wait_ge(sem("sb_z"), h + 1)
                if h >= 2:
                    dve.wait_ge(sem("sb_v"), h - 1)
                dve.tensor_scalar(sbt[:, h % 2, :], ps[:, W0 + h % 2, 0:384], 30.0, None, ALU.min).then_inc(sem("sb_m"), 1)

            def sb_second(h):
                dve.wait_ge(sem("sb_l"), h + 1)
                dve.tensor_tensor(sbn[:, h % 2, :], sbt[:, h % 2, :], ps[:, W0 + h % 2, 0:384],
                                  ALU.max).then_inc(sem("sb_n"), 1)

            def sb_split(p):
                dve.wait_ge(sem("sb_hi"), p + 1)
                dve.tensor_tensor(Y[1][:, 0, p, :], ps[:, W2 + p % 2, 0:S], Y[0][:, 0, p, :].bitcast(F32),
                                  ALU.subtract).then_inc(sem("sb_lo"), 1)

            sb_first(0)
            for h in range(8):
                if h < 7:
                    sb_first(h + 1)
                sb_second(h)
                if h % 2 == 0 and h >= 2:
                    sb_split(h // 2 - 1)
            sb_split(3)
            for n in range(16):
                if n % 4 == 0:
                    lo(base + n3 + n // 4 + LEAD)
                att_step(3, n, lambda h, t: chunked[t])
                if n == 9:
                    att_close(3, 0, y3)
            att_close(3, 1, y3)
            y_lo(4, 1)
            for u in range(4, 8):
                lo(base + n3 + u + LEAD)
            p0 = 2 * pair_of["wob"]
            residual(p0, 2 - p0, last_unit("wob"))
            norm(5)
            mlp(2)
            norm(6)


def constants():
    i = np.arange(P)
    c = np.zeros((P, N_CONST), np.float32)

    def put(col, v):
        c[:, col:col + v.shape[1]] = v

    put(C_ID, np.eye(P))
    put(C_FLIP, np.eye(P)[::-1])
    put(C_TRI, i[:, None] <= i[None, :])
    put(C_ONE, np.ones((P, P)))
    put(C_NSUF, np.where(i[:, None] >= i[None, :], -1.0, 0.0))
    put(C_NONE, -np.ones((P, P)))
    put(C_CM, np.where(i[None, :] <= i[:, None], 0.0, NEG))
    put(C_CK, np.where(i[None, :] // 64 <= i[:, None] // 64, 0.0, NEG))
    put(C_ST, np.where(i[:, None] < i[None, :], 0.0, NEG))
    put(C_BD, (i[:, None] // HB == i[None, :] // HB) & (i[:, None] <= i[None, :]))
    dist = np.maximum(255 - np.arange(384), 0)
    far = 16 + (np.log(np.maximum(dist, 1).astype(np.float32) / np.float32(16)) / np.float32(np.log(8.0))
                * np.float32(16)).astype(np.int32)
    bucket = np.where(dist < 16, dist, np.minimum(far, 31))
    c[:32, C_OH:C_OH + 384] = np.arange(32)[:, None] == bucket[None, :]
    put(C_FREQ, np.broadcast_to(np.float32(10000.0) ** (-np.arange(16, dtype=np.float32) / np.float32(16)), (P, 16)))
    put(C_BLK, i[:, None] // HB == np.arange(4)[None, :])
    return c


def units_of(w, kind, kpu):
    k, cols = w.shape
    w = w.reshape(k // P, P, cols)
    if kind == "F":
        return np.ascontiguousarray(w.reshape(k // P, P, cols // P, P).transpose(2, 1, 0, 3)).reshape(cols // P, P, -1)
    n = -(-(k // P) // kpu)
    out = np.zeros((n, P, UNIT), w.dtype)
    for j in range(n):
        part = w[j * kpu:(j + 1) * kpu].transpose(1, 0, 2)
        out[j, :, :part.shape[1] * cols] = part.reshape(P, -1)
    return out


def layout(a):
    w = a["w_in"][0]
    b = a["w_in_ab_2"][0]
    c = a["w_in_cd_2"][0]
    ukv = a["w_ukv_2"][0].reshape(256, 8, 128)
    mats = {
        "aq": np.ascontiguousarray(w[:, 0:512].reshape(D, 2, 4, 64).transpose(0, 2, 1, 3)).reshape(D, 512), "akv": np.concatenate([w[:, 512:768], w[:, 1088:1092]], 1),
        "iqk": np.concatenate([w[:, 768:1088], w[:, 1024:1088]], 1),
        "hq": w[:, 1092:1604], "hf": w[:, 1604:2116], "hi": w[:, 2116:2628], "hg": w[:, 2628:3140],
        "cb": w[:, 3140:3652], "cc": w[:, 3652:4164], "ch": w[:, 4164:4676],
        "fq": b[:, 0:512], "fk": b[:, 512:1024], "fv": b[:, 1024:1536], "fa": b[:, 1536:1544],
        "bq": b[:, 1544:2056], "bk": b[:, 2056:2568], "bv": b[:, 2568:3080],
        "sq": c[:, 0:512], "sk": c[:, 512:1024], "sv": c[:, 1024:1536], "cq": c[:, 1536:1920],
        "ckv": c[:, 1920:2208], "uq0": a["w_uq_2"][0][:, 0:512], "uq1": a["w_uq_2"][0][:, 512:768],
        "kn": ukv[:, :, 0:64].reshape(256, 512), "vn": ukv[:, :, 64:128].reshape(256, 512),
        "wo0": a["w_out"][0][:, 0:512], "wo1": a["w_out"][0][:, 512:1024],
    }
    ups = (a["w_up_attn"][0], a["w_up_hgrn"][0], a["w_up_conv"][0])
    for i in range(3):
        for h in range(2):
            mats[f"g{i}{h}"] = w[:, 4676 + 1024 * i + 512 * h:4676 + 1024 * i + 512 * (h + 1)]
            mats[f"u{i}{h}"] = ups[i][:, 512 * h:512 * (h + 1)]
    mlps = ((a["w_mlp_up"][0], a["w_mlp_down"][0]), (a["w_up_2"][0], a["w_down_2"][0]), (a["w_up_2"][1], a["w_down_2"][1]))
    parts = []
    for name, j in JOBS.items():
        if j["kind"] in "TF":
            parts.append(units_of(mats[name], j["kind"], j["kpu"]))
        elif j["kind"] == "O":
            wo = a["w_out_ab_2" if name == "woa" else "w_out_cd_2"][0]
            for kh in range(2):
                for half in range(2):
                    parts.append(units_of(wo[512 * kh:512 * (kh + 1), 512 * half:512 * (half + 1)], "T", 2))
        else:
            up, down = mlps[int(name[3:])]
            ups_ = [units_of(up[:, GROUP * g:GROUP * (g + 1)], "F", KT) for g in range(NG)]
            downs = [np.concatenate([units_of(down[GROUP * g:GROUP * (g + 1), 512 * h:512 * (h + 1)], "T", 2)
                                     for h in range(2)]) for g in range(NG)]
            parts.append(ups_[0])
            for g in range(1, NG):
                parts += [ups_[g], downs[g - 1]]
            parts.append(downs[NG - 1])
    stream = np.concatenate(parts)

    s = np.zeros((P, N_SMALL), np.float32)

    def column(col, v):
        v = v.reshape(-1, P).transpose()
        s[:, col:col + v.shape[1]] = v

    column(G_MIX, a["ln_mix_g"])
    column(G_MLP, a["ln_mlp_g"])
    column(G_N2, a["norm_mix_2"])
    column(G_M2, a["norm_mlp_2"])
    column(G_Q, np.concatenate([a["q_norm_g"][0]] * 2))
    column(G_K, np.concatenate([a["k_norm_g"][0]] * 2))
    s[:, G_CONV:G_CONV + 12] = a["conv_w"][0].reshape(3, 4, P).transpose(2, 1, 0).reshape(P, 12)
    column(G_CQ, a["q_norm_2"])
    column(G_CKV, a["kv_norm_2"])
    s[:, G_H:G_H + P] = a["hgrn_norm_g"]
    s[:, G_BF:G_BF + 8] = a["b_forget_2"]
    rb2 = np.zeros((8, 400), np.float32)
    rb2[:, 0:319] = a["rel_bias_2"][0][:, 318::-1]
    return {"stream": stream, "const": constants(), "small": s,
            "pos": np.ascontiguousarray(a["positions_2"].reshape(TT, P).transpose()),
            "relb": np.ascontiguousarray(a["rel_bias"]), "rb2": rb2, "gfin": np.ascontiguousarray(a["norm_final_2"]),
            "x_in": np.ascontiguousarray(a["x"][0])}


def kernel(**inputs):
    import concourse.bacc as bacc
    from concourse.bass_utils import run_bass_kernel_spmd

    nc = bacc.Bacc("TRN2", target_bir_lowering=False, num_devices=1, dynamic_dma_scratch_size=1024)
    arrays = layout({k: np.asarray(v) for k, v in inputs.items()})
    args = [nc.dram_tensor(k, v.shape, mybir.dt.from_np(v.dtype), kind="ExternalInput").ap() for k, v in arrays.items()]
    args.append(nc.dram_tensor("scratch", (8, 400), F32).ap())
    args.append(nc.dram_tensor("out", (S, D), F32, kind="ExternalOutput").ap())
    model(nc, *args)
    r = run_bass_kernel_spmd(nc, [arrays], core_ids=[0])
    return r.results[0]["out"].reshape(1, S, D)
```
